# Optimizing a Trainium2 kernel written in Bass

```python
import jax, jax.numpy as jnp
from jax import lax
import numpy as np

D_MODEL = 1024
BATCH = 1
SEQ = 256
DEPTH = 1
DEC_BATCH = 1
DEC_SEQ = 512
PAST_LEN = 128

GRID_W = 64
N_MEM = 256
ATT_HEADS = 8
ATT_KV_HEADS = 2
HEAD_DIM = 64
ATT_WIDTH = ATT_HEADS * HEAD_DIM
KV_WIDTH = ATT_KV_HEADS * HEAD_DIM
Q_BLOCK = 128
ROPE_THETA = 10000.0
ROPE_AXIS_DIM = HEAD_DIM // 2
CONV_WIDTH = D_MODEL - ATT_WIDTH
CONV_KSIZE = 31
MIX_WIDTH = ATT_WIDTH + CONV_WIDTH
IN_WIDTH = ATT_WIDTH + 2 * KV_WIDTH + 2 * CONV_WIDTH
MEM_HEADS = 4
MEM_HEAD_DIM = D_MODEL // MEM_HEADS
N_GROUPS = 4
EXPERTS_PER_GROUP = 8
N_EXPERTS = N_GROUPS * EXPERTS_PER_GROUP
TOP_K = 2
D_EXPERT = 256
LN_EPS = 1e-5
RMS_EPS = 1e-6
DEEPNORM_ALPHA = (2.0 * DEPTH) ** 0.25
DEEPNORM_BETA = (8.0 * DEPTH) ** -0.25

kernel_name = 'hybrid_bidir_encoder_gqa_conformer_hmoe'

def _layer_norm(x, g, b):
    xf = x.astype(jnp.float32)
    mu = jnp.mean(xf, -1, keepdims=True)
    var = jnp.mean(jnp.square(xf - mu), -1, keepdims=True)
    return ((xf - mu) * lax.rsqrt(var + LN_EPS) * g + b).astype(x.dtype)

def _rms_norm(x, g):
    xf = x.astype(jnp.float32)
    return (xf * lax.rsqrt(jnp.mean(xf * xf, -1, keepdims=True) + RMS_EPS) * g).astype(x.dtype)

def _axial_rope_tables(n_tok):
    rows = n_tok // GRID_W
    row = jnp.repeat(jnp.arange(rows, dtype=jnp.float32), GRID_W)
    col = jnp.tile(jnp.arange(GRID_W, dtype=jnp.float32), rows)
    inv_freq = ROPE_THETA ** (-jnp.arange(0, ROPE_AXIS_DIM, 2, dtype=jnp.float32) / ROPE_AXIS_DIM)
    ang = jnp.concatenate([row[:, None] * inv_freq, col[:, None] * inv_freq], -1)
    return jnp.cos(ang), jnp.sin(ang)

def _apply_rope(x, cos, sin):
    xf = x.astype(jnp.float32).reshape(x.shape[:-1] + (HEAD_DIM // 2, 2))
    x0, x1 = xf[..., 0], xf[..., 1]
    c, s = cos[None, :, None, :], sin[None, :, None, :]
    out = jnp.stack([x0 * c - x1 * s, x0 * s + x1 * c], -1)
    return out.reshape(x.shape).astype(x.dtype)

def _blocked_gqa(q, k, v):
    b, s = q.shape[:2]
    rep = ATT_HEADS // ATT_KV_HEADS
    nblk = s // Q_BLOCK
    qb = q.reshape(b, nblk, Q_BLOCK, ATT_KV_HEADS, rep, HEAD_DIM).transpose(1, 0, 2, 3, 4, 5)
    scale = HEAD_DIM ** -0.5

    def one_block(q_blk):
        sc = jnp.einsum('bqhgd,bkhd->bhgqk', q_blk, k, preferred_element_type=jnp.float32) * scale
        p = jax.nn.softmax(sc, axis=-1).astype(v.dtype)
        return jnp.einsum('bhgqk,bkhd->bqhgd', p, v)

    out = lax.map(one_block, qb)
    return out.transpose(1, 0, 2, 3, 4, 5).reshape(b, s, ATT_WIDTH)

def _depthwise_conv(u, w, bias):
    pad = CONV_KSIZE // 2
    out = lax.conv_general_dilated(u, w[:, None, :], window_strides=(1,), padding=[(pad, pad)],
                                   dimension_numbers=('NWC', 'WIO', 'NWC'), feature_group_count=CONV_WIDTH)
    return out + bias

def _parallel_mixer(h, cos, sin, w_in, q_g, k_g, conv_w, conv_b, cln_g, cln_b, w_out):
    b, s, _ = h.shape
    z = h @ w_in
    i1 = ATT_WIDTH
    i2 = i1 + KV_WIDTH
    i3 = i2 + KV_WIDTH
    i4 = i3 + CONV_WIDTH
    q, k, v, a, gate = jnp.split(z, [i1, i2, i3, i4], axis=-1)
    q = _apply_rope(_rms_norm(q.reshape(b, s, ATT_HEADS, HEAD_DIM), q_g), cos, sin)
    k = _apply_rope(_rms_norm(k.reshape(b, s, ATT_KV_HEADS, HEAD_DIM), k_g), cos, sin)
    v = v.reshape(b, s, ATT_KV_HEADS, HEAD_DIM)
    att = _blocked_gqa(q, k, v)
    u = a * jax.nn.sigmoid(gate)
    u = jax.nn.silu(_layer_norm(_depthwise_conv(u, conv_w, conv_b), cln_g, cln_b))
    return jnp.concatenate([att, u], -1) @ w_out

def _memory_xattn(h, mem, w_q, w_k, w_v, w_o):
    b, s, _ = h.shape
    m = mem.shape[1]
    q = (h @ w_q).reshape(b, s, MEM_HEADS, MEM_HEAD_DIM)
    k = (mem @ w_k).reshape(b, m, MEM_HEADS, MEM_HEAD_DIM)
    v = (mem @ w_v).reshape(b, m, MEM_HEADS, MEM_HEAD_DIM)
    sc = jnp.einsum('bqhd,bkhd->bhqk', q, k, preferred_element_type=jnp.float32) * (MEM_HEAD_DIM ** -0.5)
    p = jax.nn.softmax(sc, axis=-1).astype(v.dtype)
    o = jnp.einsum('bhqk,bkhd->bqhd', p, v).reshape(b, s, D_MODEL)
    return o @ w_o

def _hier_moe(h, w_rg, b_rg, w_re, b_re, w_gate, w_up, w_down):
    b, s, d = h.shape
    t = h.reshape(b * s, d)
    g_logits = (t @ w_rg).astype(jnp.float32) + b_rg
    g_prob = jax.nn.softmax(g_logits, axis=-1)
    grp_1h = jax.nn.one_hot(jnp.argmax(g_logits, -1), N_GROUPS, dtype=jnp.float32)
    p_grp = jnp.sum(g_prob * grp_1h, -1, keepdims=True)
    e_logits = jnp.einsum('td,gde->tge', t, w_re).astype(jnp.float32) + b_re
    e_logits = jnp.einsum('tg,tge->te', grp_1h, e_logits)
    top_v, top_i = lax.top_k(e_logits, TOP_K)
    top_w = jax.nn.softmax(top_v, axis=-1) * p_grp
    within = jnp.sum(jax.nn.one_hot(top_i, EXPERTS_PER_GROUP, dtype=jnp.float32) * top_w[..., None], 1)
    comb = (grp_1h[:, :, None] * within[:, None, :]).reshape(-1, N_EXPERTS).astype(t.dtype)
    y = jnp.zeros_like(t)
    for e in range(N_EXPERTS):
        he = jax.nn.silu(t @ w_gate[e]) * (t @ w_up[e])
        y = y + comb[:, e:e + 1] * (he @ w_down[e])
    return y.reshape(b, s, d)

def _encoder(x, mem, ln_in_g, ln_in_b, ln_mem_g, ln_mem_b, w_in, q_norm_g, k_norm_g, conv_w, conv_b,
             conv_ln_g, conv_ln_b, w_mix_out, ln1_g, ln1_b, w_cq, w_ck, w_cv, w_co, ln2_g, ln2_b,
             w_router_g, b_router_g, w_router_e, b_router_e, w_e_gate, w_e_up, w_e_down, ln3_g, ln3_b):
    cos, sin = _axial_rope_tables(x.shape[1])
    h = _layer_norm(x, ln_in_g, ln_in_b)
    m = _layer_norm(mem, ln_mem_g, ln_mem_b)
    for l in range(DEPTH):
        mix = _parallel_mixer(h, cos, sin, w_in[l], q_norm_g[l], k_norm_g[l], conv_w[l], conv_b[l],
                              conv_ln_g[l], conv_ln_b[l], w_mix_out[l])
        h = _layer_norm(DEEPNORM_ALPHA * h + mix, ln1_g[l], ln1_b[l])
        xa = _memory_xattn(h, m, w_cq[l], w_ck[l], w_cv[l], w_co[l])
        h = _layer_norm(DEEPNORM_ALPHA * h + xa, ln2_g[l], ln2_b[l])
        ff = _hier_moe(h, w_router_g[l], b_router_g[l], w_router_e[l], b_router_e[l],
                       w_e_gate[l], w_e_up[l], w_e_down[l])
        h = _layer_norm(DEEPNORM_ALPHA * h + ff, ln3_g[l], ln3_b[l])
    return h

def setup_inputs(seed: int = 0) -> dict:
    key = jax.random.key(seed)
    ks = iter(jax.random.split(key, 40))
    f32 = jnp.float32

    def nrm(shape, scale):
        return jax.random.normal(next(ks), shape, f32) * scale

    def gain(shape):
        return 1.0 + nrm(shape, 0.02)

    d = D_MODEL
    col_scale = jnp.concatenate([
        jnp.ones((ATT_WIDTH + KV_WIDTH,), f32),
        jnp.full((KV_WIDTH + 2 * CONV_WIDTH,), DEEPNORM_BETA, f32)])
    return {
        'x_prompt': nrm((BATCH, SEQ, d), 1.0),
        'x_sample': nrm((DEC_BATCH, DEC_SEQ, d), 1.0),
        'mem_prompt': nrm((BATCH, N_MEM, d), 1.0),
        'mem_sample': nrm((DEC_BATCH, N_MEM, d), 1.0),
        'ln_in_g': gain((d,)),
        'ln_in_b': nrm((d,), 0.02),
        'ln_mem_g': gain((d,)),
        'ln_mem_b': nrm((d,), 0.02),
        'w_in': nrm((DEPTH, d, IN_WIDTH), d ** -0.5) * col_scale,
        'q_norm_g': gain((DEPTH, HEAD_DIM)),
        'k_norm_g': gain((DEPTH, HEAD_DIM)),
        'conv_w': nrm((DEPTH, CONV_KSIZE, CONV_WIDTH), CONV_KSIZE ** -0.5),
        'conv_b': nrm((DEPTH, CONV_WIDTH), 0.02),
        'conv_ln_g': gain((DEPTH, CONV_WIDTH)),
        'conv_ln_b': nrm((DEPTH, CONV_WIDTH), 0.02),
        'w_mix_out': nrm((DEPTH, MIX_WIDTH, d), MIX_WIDTH ** -0.5 * DEEPNORM_BETA),
        'ln1_g': gain((DEPTH, d)),
        'ln1_b': nrm((DEPTH, d), 0.02),
        'w_cq': nrm((DEPTH, d, d), d ** -0.5),
        'w_ck': nrm((DEPTH, d, d), d ** -0.5),
        'w_cv': nrm((DEPTH, d, d), d ** -0.5 * DEEPNORM_BETA),
        'w_co': nrm((DEPTH, d, d), d ** -0.5 * DEEPNORM_BETA),
        'ln2_g': gain((DEPTH, d)),
        'ln2_b': nrm((DEPTH, d), 0.02),
        'w_router_g': nrm((DEPTH, d, N_GROUPS), d ** -0.5),
        'b_router_g': nrm((DEPTH, N_GROUPS), 0.01),
        'w_router_e': nrm((DEPTH, N_GROUPS, d, EXPERTS_PER_GROUP), d ** -0.5),
        'b_router_e': nrm((DEPTH, N_GROUPS, EXPERTS_PER_GROUP), 0.01),
        'w_e_gate': nrm((DEPTH, N_EXPERTS, d, D_EXPERT), d ** -0.5),
        'w_e_up': nrm((DEPTH, N_EXPERTS, d, D_EXPERT), d ** -0.5 * DEEPNORM_BETA),
        'w_e_down': nrm((DEPTH, N_EXPERTS, D_EXPERT, d), D_EXPERT ** -0.5 * DEEPNORM_BETA),
        'ln3_g': gain((DEPTH, d)),
        'ln3_b': nrm((DEPTH, d), 0.02),
    }

def reference(x_prompt, x_sample, mem_prompt, mem_sample, ln_in_g, ln_in_b, ln_mem_g, ln_mem_b, w_in,
              q_norm_g, k_norm_g, conv_w, conv_b, conv_ln_g, conv_ln_b, w_mix_out, ln1_g, ln1_b,
              w_cq, w_ck, w_cv, w_co, ln2_g, ln2_b, w_router_g, b_router_g, w_router_e, b_router_e,
              w_e_gate, w_e_up, w_e_down, ln3_g, ln3_b):
    y_prompt = _encoder(x_prompt, mem_prompt, ln_in_g, ln_in_b, ln_mem_g, ln_mem_b, w_in, q_norm_g, k_norm_g,
                        conv_w, conv_b, conv_ln_g, conv_ln_b, w_mix_out, ln1_g, ln1_b, w_cq, w_ck, w_cv, w_co,
                        ln2_g, ln2_b, w_router_g, b_router_g, w_router_e, b_router_e, w_e_gate, w_e_up,
                        w_e_down, ln3_g, ln3_b)
    y_sample = _encoder(x_sample, mem_sample, ln_in_g, ln_in_b, ln_mem_g, ln_mem_b, w_in, q_norm_g, k_norm_g,
                        conv_w, conv_b, conv_ln_g, conv_ln_b, w_mix_out, ln1_g, ln1_b, w_cq, w_ck, w_cv, w_co,
                        ln2_g, ln2_b, w_router_g, b_router_g, w_router_e, b_router_e, w_e_gate, w_e_up,
                        w_e_down, ln3_g, ln3_b)
    return (y_prompt, y_sample)


_drawn_inputs = setup_inputs


def setup_inputs(seed=0):
    import zlib

    import numpy as np

    out = dict(_drawn_inputs(seed))
    spreads = {}
    factors = {'ln_mem_g': 8.0,
     'ln_mem_b': 7.531,
     'q_norm_g': 8.0,
     'k_norm_g': 8.0,
     'conv_b': 3.79,
     'conv_ln_g': 7.765,
     'conv_ln_b': 8.0,
     'ln1_b': 2.706,
     'ln2_b': 2.683,
     'b_router_g': 33.434,
     'b_router_e': 32.056,
     'ln3_g': 8.387,
     'ln3_b': 7.935}
    for name, (base, spread) in spreads.items():
        noise = np.random.default_rng([zlib.crc32(name.encode()), seed]).standard_normal(out[name].shape)
        drawn = base * np.exp(spread * noise) if base else spread * noise
        out[name] = __import__('jax').numpy.asarray(drawn.astype(out[name].dtype))
    for name, factor in factors.items():
        out[name] = (out[name] * factor).astype(out[name].dtype)
    return out
```

```python
from contextlib import ExitStack

import concourse.bass as bass
from concourse import mybir

F32 = mybir.dt.float32
I32 = mybir.dt.int32
U32 = mybir.dt.uint32
ALU = mybir.AluOpType
ACT = mybir.ActivationFunctionType
AX = mybir.AxisListType

P = 128
D = 1024
KC = D // P
SEQS = ((0, 256), (256, 512))
T = sum(n for _, n in SEQS)
NT = T // P
TILES = [(s, i) for s, (t0, n) in enumerate(SEQS) for i in range(t0 // P, (t0 + n) // P)]
HEADS, KV_HEADS, HD = 8, 2, 64
PAIRS = HEADS // KV_HEADS
NQK = HEADS + KV_HEADS
CONV, TAPS = 512, 31
PAD = TAPS // 2
CC = CONV // P
UW = T + 4 * PAD
N_MEM = 256
MT = len(SEQS) * N_MEM // P
MHEADS, MHD = 4, 256
GROUPS, EPG = 4, 8
NE = GROUPS * EPG
FE = 256
NR = GROUPS + NE
LN_EPS, RMS_EPS = 1e-5, 1e-6
ALPHA = 2.0 ** 0.25
C = P
BLOCKS = T // C
MAX_OVER = (2 * T - 1) // C
PAIRS_OVER = (MAX_OVER + 1) // 2
NB = 4
STEADY = NE + 2
AHEAD = 3
LIST = 2 * PAIRS_OVER
BIG = 4095
SLOT = KC * 512


def weight_slabs(w_in, w_mix, w_ck, w_cv, w_cq, w_co):
    return [("a", w_in[:, 768:1280]), ("g", w_in[:, 1280:1792]), ("q", w_in[:, 0:512]), ("kv", w_in[:, 512:768]),
            ("mix0", w_mix[:, 0:512]), ("mix1", w_mix[:, 512:1024]),
            ("ck0", w_ck[:, 0:512]), ("ck1", w_ck[:, 512:1024]),
            ("cv0", w_cv[:, 0:512]), ("cv1", w_cv[:, 512:1024]),
            ("cq0", w_cq[:, 0:512]), ("cq1", w_cq[:, 512:1024]),
            ("co0", w_co[:, 0:512]), ("co1", w_co[:, 512:1024])]


def self_units():
    out, n = [], 0
    for s, (t0, length) in enumerate(SEQS):
        for pair in range(PAIRS):
            for half in range(KV_HEADS):
                for i in range(length // P):
                    out.append((n, s, pair + PAIRS * half, i, length))
                n += 1
    return out


def cross_units():
    out, n = [], 0
    for s, (t0, length) in enumerate(SEQS):
        for h in range(MHEADS):
            for i in range(length // P):
                out.append((n, s, h, i, N_MEM))
            n += 1
    return out


SELF, CROSS = self_units(), cross_units()
S_AHEAD = 3


def plan_banks():
    place, used, turn = {}, [0] * 8, {}

    def take(kind, key):
        banks = {"mm": (0, 1, 2, 3), "tr": (4, 5), "pv": (6, 7)}[kind]
        b = banks[turn.get(kind, 0) % len(banks)]
        turn[kind] = turn.get(kind, 0) + 1
        place[key] = (b, used[b])
        used[b] += 1

    take("tr", "cpar")
    for i in range(NT):
        for j in range(2):
            take("tr", ("hT", 0, i, j))
    for c in range(CC):
        for s in range(2):
            take("mm", ("a", c, s))
            take("mm", ("g", c, s))
    for i in range(NT):
        take("mm", ("q", i))
        take("mm", ("kv", i))
    for i in range(NT):
        take("tr", ("qT", i))
        take("tr", ("kT", i))
    for what in ("mean", "var"):
        for s in range(2):
            take("mm", (what, s))
    for kind, units in (("s", SELF), ("x", CROSS)):
        if kind == "x":
            for i in range(NT):
                for j in range(2):
                    take("mm", ("mix", i, j))
            for layer, i in [("m", 0), ("m", 1)] + [(1, i) for i in range(MT)] + [("m", 2), ("m", 3)]:
                for j in range(2):
                    take("tr", ("mT", i, j) if layer == "m" else ("hT", 1, i, j))
            for c in range(KC):
                take("mm", ("ck", c))
            for i in range(MT):
                for j in range(2):
                    take("mm", ("cv", i, j))
            for i in range(MT, NT):
                for j in range(2):
                    take("tr", ("hT", 1, i, j))
            for c in range(KC):
                for s in range(2):
                    take("mm", ("cq", c, s))
        for u in range(len(units)):
            take("mm", (kind + "S", u))
            take("tr", (kind + "T", u))
        for n in range(units[-1][0] + 1):
            for j in range(1 if kind == "s" else 2):
                take("pv", (kind + "O", n, j))
    for i in range(NT):
        for j in range(2):
            take("mm", ("co", i, j))
    for i in range(NT):
        for j in range(2):
            take("tr", ("hT", 2, i, j))
    take("pv", "route")
    for key in ("rank", "count", "base", "list"):
        take("mm", key)
    return place, used


def encoder(nc, x, mem, w_slabs, lnp, rope_cos, rope_sin, q_gain, k_gain, cpar_dram, w_router, b_router,
            w_gate, w_up, w_down, y):
    place, bank_uses = plan_banks()
    slab_names = [n for n, _ in w_slabs]
    h2_dram = nc.dram_tensor("h2_rows", [T, D], F32).ap()
    pair_dram = nc.dram_tensor("pair_rows", [2 * T, D], F32).ap()
    table_dram = nc.dram_tensor("slot_table", [T * NE, 2], I32).ap()

    with ExitStack() as ctx:
        def sb(name, shape, dt=F32):
            return ctx.enter_context(nc.sbuf_tensor(name, shape, dt))

        def sem(name):
            return ctx.enter_context(nc.semaphore(name))

        ps = ctx.enter_context(nc.psum_tensor("ps", [P, 8, 512], F32))

        hres = sb("hres", [P, NT, D])
        hT = sb("hT", [P, KC * T])
        cat = sb("cat", [P, KC * T])
        early = sb("early", [P, 8192])
        scr = sb("scr", [P, 6144])
        ring = sb("ring", [P, 3, SLOT])
        gb = sb("gb", [P, 2, D])
        memx = sb("memx", [P, 2 * D])

        hTv = hT[:, :].rearrange("p (k t) -> p k t", k=KC)
        catv = cat[:, :].rearrange("p (k t) -> p k t", k=KC)
        upad = early[:, 0:CC * UW].rearrange("p (c t) -> p c t", c=CC)
        o = CC * UW
        qT = early[:, o:o + PAIRS * T].rearrange("p (c t) -> p c t", c=PAIRS)
        o += PAIRS * T
        kT = early[:, o:o + T]
        o += T
        vtok = early[:, o:o + NT * P].rearrange("p (i c) -> p i c", i=NT)
        assert o + NT * P <= 8192
        kmT = early[:, 0:4096].rearrange("p (k t) -> p k t", k=KC)
        vm = early[:, 4096:8192].rearrange("p (i c) -> p i c", i=MT)
        sig = scr[:, 0:CC * T].rearrange("p (c t) -> p c t", c=CC)
        raw = [scr[:, CC * T + 640 * n:CC * T + 640 * (n + 1)].rearrange("p (h d) -> p h d", h=NQK) for n in range(2)]
        rtmp = [scr[:, CC * T + 1280 + 320 * n:CC * T + 1280 + 320 * (n + 1)].rearrange("p (h d) -> p h d", h=NQK)
                for n in range(2)]
        cos_raw = scr[:, CC * T + 2560:CC * T + 2688].rearrange("p (i d) -> p i d", i=4)
        sin_raw = scr[:, CC * T + 2688:CC * T + 2816].rearrange("p (i d) -> p i d", i=4)
        squares = [(scr[:, CC * T + 1920:CC * T + 2560]), memx[:, 1280:1920]]
        rot = [memx[:, 640 * n:640 * (n + 1)] for n in range(2)]
        convsq = scr[:, 0:CC * T].rearrange("p (c t) -> p c t", c=CC)
        crstd = scr[:, CC * T:CC * T + T]
        PT = [scr[:, 2048 * n:2048 * (n + 1)].rearrange("p (k t) -> p k t", k=4) for n in range(2)]
        prob = [scr[:, 4096 + 512 * n:4096 + 512 * (n + 1)] for n in range(4)]
        mT = scr[:, 0:4096].rearrange("p (k t) -> p k t", k=KC)
        mgb = scr[:, 4096:6144].rearrange("p (a d) -> p a d", a=2)
        mrow = [memx[:, D * n:D * (n + 1)] for n in range(2)]
        acc = catv[:, CC:2 * CC, :]
        ringf = ring[:, :, :].rearrange("p n c -> p (n c)")
        wexp = [early[:, 0:6144], scr[:, 0:6144], ringf[:, 0:6144], cat[:, 0:6144]]
        xg = [hT[:, D * n:D * (n + 1)] for n in range(2)] + [ringf[:, 6144 + D * n:6144 + D * (n + 1)] for n in range(2)]
        xT = [hT[:, D * (2 + n):D * (3 + n)].rearrange("p (k t) -> p k t", k=KC) for n in range(2)]
        yo = [hT[:, D * (4 + n):D * (5 + n)] for n in range(2)]
        hid = [memx[:, 256 * n:256 * (n + 1)].rearrange("p (k t) -> p k t", k=2) for n in range(2)]
        act_g = [memx[:, 512 + 256 * n:512 + 256 * (n + 1)].rearrange("p (k t) -> p k t", k=2) for n in range(2)]
        prow = [cat[:, D * n:D * (n + 1)] for n in range(6)]

        ident = sb("ident", [P, P])
        ones = sb("ones", [P, P])
        ones_c = sb("ones_c", [P, P])
        before = sb("before", [P, P])
        qtab = sb("qtab", [P, 4, 4, 32])
        ktab = sb("ktab", [P, 4, 4, 32])
        qkg = sb("qkg", [P, 2, HD])
        cpar_in = sb("cpar_in", [TAPS + 3, CONV])
        cpar = sb("cpar", [P, CC, TAPS + 3])
        epsv = sb("epsv", [P, 2])
        stats = sb("stats", [P, 2, 2, 6])
        mv = sb("mv", [P, 2, 2])
        lnc = sb("lnc", [P, 2, 2])
        lnt = sb("lnt", [P, 1])
        ssq = sb("ssq", [P, NT, NQK])
        rqk = sb("rqk", [P, 2, NQK])
        mhalf = sb("mhalf", [P, NQK])
        nmax = sb("nmax", [P, 4])
        rsum = sb("rsum", [P, 4])
        rinv = sb("rinv", [P, 4])
        wr = sb("wr", [P, KC, NR])
        br = sb("br", [P, NR])[:, :]
        tinit = sb("tinit", [P, T * NE // P * 2], I32)
        tvals = sb("tvals", [P, NT, 2, 2], I32)
        slots = sb("slots", [P, 2, NT], U32)
        tab = sb("tab", [P, BLOCKS * NE * 2 + 2], I32)
        gidx = [sb(f"gidx{n}", [P, 1], U32) for n in range(NB)]
        sidx = [sb(f"sidx{n}", [P, 1], U32) for n in range(2)]
        ctl = sb("ctl", [1, 1 + 2 * LIST], I32)
        pw = sb("pw", [P, 2, NT])

        rt, at = ring[:, 2, :], [0]

        def rv(*shape):
            n = 1
            for k in shape:
                n *= k
            a = rt[:, at[0]:at[0] + n]
            at[0] += n
            if len(shape) == 2:
                return a.rearrange("p (a b) -> p a b", a=shape[0])
            if len(shape) == 3:
                return a.rearrange("p (a b c) -> p a b c", a=shape[0], b=shape[1])
            return a

        lg = rv(NT, NR)
        gmx, gm2, gsum, pgrp = rv(NT), rv(NT), rv(NT), rv(NT)
        geq, G, gex = rv(NT, GROUPS), rv(NT, GROUPS), rv(NT, GROUPS)
        esel4, esel = rv(NT, GROUPS, EPG), rv(NT, EPG)
        v1, v2, m1, m2, ev, den = rv(NT), rv(NT), rv(NT), rv(NT), rv(NT), rv(NT)
        eq, H1, e2, H2 = rv(NT, EPG), rv(NT, EPG), rv(NT, EPG), rv(NT, EPG)
        pick = [rv(NT, GROUPS, EPG), rv(NT, GROUPS, EPG)]
        both = rv(NT, NE)
        rk, rkp = rv(NT, NE), rv(NT, NE)
        slotf = rv(NT)
        desc = rv(EPG)
        eiota = rv(NE)
        cnt, over, base = rv(1), rv(1), rv(1)
        thr = rv(BLOCKS - 1)
        more = rv(BLOCKS - 1)
        jb = rv(BLOCKS - 1, LIST)
        hitm = rv(BLOCKS - 1, LIST)
        bcol = rv(BLOCKS - 1)
        lst = rv(2 * (BLOCKS - 1) * LIST)
        lstb = rv((BLOCKS - 1) * LIST)
        res = rv(1 + 2 * LIST)
        ecol = rv(2)
        assert at[0] <= SLOT

        bank_full = [sem(f"bank_full{b}") for b in range(8)]
        bank_free = [sem(f"bank_free{b}") for b in range(8)]
        slab_in = [sem(f"slab_in{n}") for n in range(3)]
        x_in = [sem(f"x_in{n}") for n in range(NT)]
        mem_in = [sem(f"mem_in{n}") for n in range(2)]
        gb_in, mgb_in, conv_in, small_in, rope_in = sem("gb_in"), sem("mgb_in"), sem("conv_in"), sem("small_in"), sem("rope_in")
        const_pool, const_ready = sem("const_pool"), sem("const_ready")
        ln_stats, ln_coef, ln_hat, ln_gain, ln_done = (sem(n) for n in
                                                       ("ln_stats", "ln_coef", "ln_hat", "ln_gain", "ln_done"))
        dve_step, act_step, pool_step = sem("dve_step"), sem("act_step"), sem("pool_step")
        hT_ready, cpar_ready = sem("hT_ready"), sem("cpar_ready")
        u_ready, conv_done, qkv_raw, rot_ready = sem("u_ready"), sem("conv_done"), sem("qkv_raw"), sem("rot_ready")
        tabs_ready = sem("tabs_ready")
        qkT_ready, conv_sq, conv_rs, conv_out = sem("qkT_ready"), sem("conv_sq"), sem("conv_rs"), sem("conv_out")
        conv_cent, conv_norm, conv_sd = sem("conv_cent"), sem("conv_norm"), sem("conv_sd")
        max_ready, exp_done, inv_ready, prob_ready, PT_ready, heads_done, out_ready = (
            sem(n) for n in ("max_ready", "exp_done", "inv_ready", "prob_ready", "PT_ready", "heads_done", "out_ready"))
        res_ready, mT_ready, memkv_ready, cq_ready = sem("res_ready"), sem("mT_ready"), sem("memkv_ready"), sem("cq_ready")
        cq_used = sem("cq_used")
        h2_stored, route_exp, route_const, route_dve = sem("h2_stored"), sem("route_exp"), sem("route_const"), sem("route_dve")
        table_init, slots_ready, table_done, tab_in = sem("table_init"), sem("slots_ready"), sem("table_done"), sem("tab_in")
        counts_in, ctl_ready, rank_used = sem("counts_in"), sem("ctl_ready"), sem("rank_used")
        wexp_in = [sem(f"wexp_in{n}") for n in range(NB)]
        rows_in = [sem(f"rows_in{n}") for n in range(NB)]
        rows_out = [sem(f"rows_out{n}") for n in range(2)]
        gidx_ready, sidx_ready, index_seen = sem("gidx_ready"), sem("sidx_ready"), sem("index_seen")
        rowsT_full, rowsT_a, rowsT_d = sem("rowsT_full"), sem("rowsT_a"), sem("rowsT_d")
        gu_full, silu_done, hid_ready, down_full, yo_a, yo_d = (
            sem(n) for n in ("gu_full", "silu_done", "hid_ready", "down_full", "yo_a", "yo_d"))
        prow_in = [sem(f"prow_in{n}") for n in range(6)]
        prow_used, y_out, scaled = sem("prow_used"), sem("y_out"), sem("scaled")

        block = ctx.enter_context(nc.Block())

        def full(eng, key):
            b, n = place[key]
            eng.wait_ge(bank_full[b], n + 1)
            return ps[:, b, :]

        def was_read(eng, key):
            b, n = place[key]
            eng.wait_ge(bank_free[b], n + 1)

        def later(n):
            return not isinstance(n, int) or n >= 1

        def free(key):
            return bank_free[place[key][0]]

        slab_last = {"a": ("a", CC - 1, 1), "g": ("g", CC - 1, 1), "q": ("q", NT - 1), "kv": ("kv", NT - 1)}
        for j in range(2):
            slab_last |= {f"mix{j}": ("mix", NT - 1, j), f"ck{j}": ("ck", 4 * j + 3), f"cv{j}": ("cv", MT - 1, j),
                          f"cq{j}": ("cq", 4 * j + 3, 1), f"co{j}": ("co", NT - 1, j)}

        LN_X = list(range(NT))
        LN_1 = [NT + n for n in (0, 2, 4, 5, 6, 7)]
        LN_M = [NT + n for n in (1, 3, 8, 9)]
        LN_2 = [LN_M[-1] + 1 + i for i in range(NT)]
        LN_3 = [LN_2[-1] + 1 + i for i in range(NT)]

        @block.sync
        def _(sp):
            def bcast(v):
                return v.rearrange("(a d) -> a d", a=1).to_broadcast([P, v.shape[0]])

            def load_gb(n):
                sp.dma_start(gb[:, 0, :], bcast(lnp[2 * n])).then_inc(gb_in, 16)
                sp.dma_start(gb[:, 1, :], bcast(lnp[2 * n + 1])).then_inc(gb_in, 16)

            def load_slab(n):
                w = w_slabs[n][1]
                if n >= 3:
                    full(sp, slab_last[slab_names[n - 3]])
                dst = ring[:, n % 3, 0:KC * w.shape[1]].rearrange("p (k c) -> p k c", k=KC)
                sp.dma_start(dst, w.rearrange("(k p) c -> p k c", p=P)).then_inc(slab_in[n % 3], 16)

            sp.dma_start(hres[:, 0, :], x[0:P, :]).then_inc(x_in[0], 16)
            load_gb(0)
            for i in range(1, NT):
                sp.dma_start(hres[:, i, :], x[i * P:(i + 1) * P, :]).then_inc(x_in[i], 16)
            sp.dma_start(cpar_in[:, :], cpar_dram).then_inc(conv_in, 16)
            sp.dma_start(qkg[:, 0, :], bcast(q_gain)).then_inc(rope_in, 16)
            sp.dma_start(qkg[:, 1, :], bcast(k_gain)).then_inc(rope_in, 16)
            sp.dma_start(cos_raw, rope_cos.rearrange("(i p) d -> p i d", p=P)).then_inc(rope_in, 16)
            sp.dma_start(sin_raw, rope_sin.rearrange("(i p) d -> p i d", p=P)).then_inc(rope_in, 16)
            for n in range(3):
                load_slab(n)
            sp.dma_start(wr[:, :, :], w_router).then_inc(small_in, 16)
            sp.dma_start(br, bcast(b_router)).then_inc(small_in, 16)
            sp.wait_ge(const_ready, 2)
            sp.dma_start(table_dram.rearrange("(p n) t -> p (n t)", p=P), tinit[:, :]).then_inc(table_init, 16)
            sp.wait_ge(ln_done, NT)
            load_gb(1)
            for n in range(3, 6):
                load_slab(n)
            full(sp, ("kT", NT - 1))
            for i in range(2):
                sp.dma_start(mrow[i], mem[i * P:(i + 1) * P, :]).then_inc(mem_in[i], 16)
            full(sp, ("sO", SELF[-1][0], 0))
            for j in range(2):
                sp.dma_start(mgb[:, j, :], bcast(lnp[2 + 6 + j])).then_inc(mgb_in, 16)
            load_slab(6)
            for i in range(2, MT):
                full(sp, ("mT", i - 2, 1))
                sp.dma_start(mrow[i % 2], mem[i * P:(i + 1) * P, :]).then_inc(mem_in[i % 2], 16)
            for n in range(7, 9):
                load_slab(n)
            sp.wait_ge(ln_done, LN_1[-1] + 1)
            load_gb(2)
            for n in range(9, len(w_slabs)):
                load_slab(n)
            full(sp, ("xO", CROSS[-1][0], 1))

            def load_expert(b, e):
                for off, w in ((0, w_gate), (2048, w_up)):
                    sp.dma_start(wexp[b][:, off:off + 2048],
                                 w[bass.ds(e, 1)].rearrange("e (p k) f -> p (e k f)", p=P)).then_inc(wexp_in[b], 16)
                sp.dma_start(wexp[b][:, 4096:6144],
                             w_down[bass.ds(e, 1)].rearrange("e (p k) f -> p (e k f)", p=P)).then_inc(wexp_in[b], 16)

            for e in range(2):
                load_expert(e, e)
            for i in range(NT):
                sp.wait_ge(ln_done, LN_2[i] + 1)
                sp.dma_start(h2_dram[i * P:(i + 1) * P, :], hres[:, i, :]).then_inc(h2_stored, 16)
            full(sp, ("co", NT - 1, 1))
            load_expert(2, 2)
            load_gb(3)
            full(sp, "route")
            load_expert(3, 3)
            sp.wait_ge(table_done, 16 * 2 * NT)
            sp.dma_start(tab[:, 0:BLOCKS * NE * 2].rearrange("p (b c) -> p b c", b=BLOCKS), table_dram.rearrange("(b p e) t -> p b (e t)", p=P, b=BLOCKS)).then_inc(tab_in, 16)
            with sp.Fori(1, NE // NB) as i:
                for b in range(NB):
                    sp.wait_ge(down_full, NB * i + b - NB + 1)
                    load_expert(b, NB * i + b)
            sp.wait_ge(ctl_ready, 1)
            for b in range(2):
                e = sp.value_load(ctl[0:1, 1 + b:2 + b], min_val=0, max_val=NE - 1)
                sp.wait_ge(down_full, NE - NB + b + 1)
                load_expert(b, e)
            n_over = sp.value_load(ctl[0:1, 0:1], min_val=0, max_val=LIST)
            with sp.Fori(1, PAIRS_OVER) as i:
                with sp.If(2 * i < n_over):
                    for b in range(2):
                        e = sp.value_load(ctl[0:1, bass.ds(1 + 2 * i + b, 1)], min_val=0, max_val=NE - 1)
                        sp.wait_ge(down_full, NE + 2 * i + b - 1)
                        load_expert(b, e)
            sp.wait_ge(prow_used, 1)
            for i in range(NT):
                for k in range(2):
                    n = 2 * (i % 3) + k
                    if i >= 3:
                        sp.wait_ge(ln_stats, LN_3[i - 3] + 1)
                    r = k * T + i * P
                    sp.dma_start(prow[n], pair_dram[r:r + P, :]).then_inc(prow_in[n], 16)
            for i in range(NT):
                sp.wait_ge(ln_done, LN_3[i] + 1)
                sp.dma_start(y[i * P:(i + 1) * P, :], hres[:, i, :]).then_inc(y_out, 16)
            sp.wait_ge(y_out, 16 * NT)

        def ln_rows(n):
            if n in LN_M:
                return mrow[LN_M.index(n) % 2], mgb[:, 0, :], mgb[:, 1, :]
            for ns in (LN_X, LN_1, LN_2, LN_3):
                if n in ns:
                    return hres[:, ns.index(n), :], gb[:, 0, :], gb[:, 1, :]

        def gb_wait(eng, n):
            if n in LN_M:
                eng.wait_ge(mgb_in, 32)
            else:
                eng.wait_ge(gb_in, 32 * (1 + [n in ns for ns in (LN_X, LN_1, LN_2, LN_3)].index(True)))

        def pool_coef(pool, n, link):
            pool.wait_ge(ln_stats, n + 1)
            if n >= 2:
                pool.wait_ge(ln_hat, n - 1)
            link(nc.gpsimd.tensor_scalar(lnt[:, :], mv[:, n % 2, 1:2], LN_EPS, None, ALU.add))
            link(nc.gpsimd.tensor_tensor(lnc[:, n % 2, 0:1], lnt[:, :], mhalf[:, 0:1], ALU.pow))
            nc.gpsimd.tensor_scalar(lnc[:, n % 2, 1:2], mv[:, n % 2, 0:1], lnc[:, n % 2, 0:1], -1.0,
                                    ALU.mult, ALU.mult).then_inc(ln_coef, 1)

        def pool_gain(pool, n):
            rows, g, _ = ln_rows(n)
            gb_wait(pool, n)
            pool.wait_ge(ln_hat, n + 1)
            nc.gpsimd.tensor_tensor(rows, rows, g, ALU.mult).then_inc(ln_gain, 1)

        def act_hat(act, n):
            rows, _, _ = ln_rows(n)
            act.wait_ge(ln_coef, n + 1)
            nc.scalar.activation(rows, rows, ACT.Identity, bias=lnc[:, n % 2, 1:2],
                                 scale=lnc[:, n % 2, 0:1]).then_inc(ln_hat, 1)

        def dve_stats(dve, n, link):
            rows, _, _ = ln_rows(n)
            if n >= 2:
                dve.wait_ge(ln_coef, n - 1)
            for j in range(2):
                last = nc.vector.bn_stats(stats[:, n % 2, j, :], rows[:, 512 * j:512 * (j + 1)])
            link(last)
            nc.vector.bn_aggr(mv[:, n % 2, :], stats[:, n % 2, :, :]).then_inc(ln_stats, 1)

        def dve_bias(dve, n):
            rows, _, b = ln_rows(n)
            gb_wait(dve, n)
            dve.wait_ge(ln_gain, n + 1)
            nc.vector.tensor_tensor(rows, rows, b, ALU.add).then_inc(ln_done, 1)

        @block.gpsimd
        def _(pool):
            steps = [0]

            def link(ins):
                steps[0] += 1
                ins.then_inc(pool_step, 1)
                pool.wait_ge(pool_step, steps[0])

            g = nc.gpsimd
            link(g.memset(mhalf[:, :], -0.5))
            g.memset(ones[:, :], 1.0).then_inc(const_pool, 1)
            g.memset(ident[:, :], 0.0).then_inc(const_pool, 1)
            g.memset(ones_c[:, :], 1.0 / CONV).then_inc(const_pool, 1)
            g.memset(epsv[:, :], LN_EPS).then_inc(const_pool, 1)
            pool.wait_ge(const_pool, 4)
            g.affine_select(out=ident[:, :], in_=ident[:, :], compare_op=ALU.not_equal, fill=1.0, base=0,
                            pattern=[[-1, P]], channel_multiplier=1).then_inc(const_pool, 1)
            g.affine_select(out=before[:, :], in_=ones[:, :], compare_op=ALU.is_gt, fill=0.0, base=0,
                            pattern=[[1, P]], channel_multiplier=-1).then_inc(const_pool, 1)
            pool.wait_ge(const_pool, 6)
            g.memset(upad, 0.0).then_inc(const_ready, 1)
            g.iota(tvals[:, :, :, 0], pattern=[[P, NT], [0, 2]], base=0, channel_multiplier=1).then_inc(const_pool, 1)
            g.iota(tvals[:, :, :, 1], pattern=[[P, NT], [T, 2]], base=0, channel_multiplier=1).then_inc(const_pool, 1)
            pool.wait_ge(const_pool, 8)
            link(g.iota(tab[:, BLOCKS * NE * 2:], pattern=[[0, 2]], base=BIG, channel_multiplier=0))
            g.iota(tinit[:, :], pattern=[[0, T * NE // P * 2]], base=BIG, channel_multiplier=0).then_inc(const_ready, 1)

            def norms(ns, lag=1):
                for k, n in enumerate(ns):
                    pool_coef(pool, n, link)
                    if k >= lag:
                        pool_gain(pool, ns[k - lag])
                for n in ns[-lag:]:
                    pool_gain(pool, n)

            norms(LN_X)

            pool.wait_ge(rope_in, 64)
            for tabx, gi in ((qtab, 0), (ktab, 1)):
                for m, (src, odd) in enumerate(((cos_raw, 0), (sin_raw, 1), (sin_raw, 0), (cos_raw, 1))):
                    gain = qkg[:, gi:gi + 1, odd:HD:2].to_broadcast([P, 4, 32])
                    last = g.tensor_tensor(tabx[:, :, m, :], src, gain, ALU.mult)
                    link(last)

            for i, (s, _) in enumerate(TILES):
                pos = i - SEQS[s][0] // P
                r = raw[i % 2]
                pool.wait_ge(qkv_raw, i + 1)
                link(g.tensor_scalar(rqk[:, 0, :], ssq[:, i, :], 1.0 / HD, RMS_EPS, ALU.mult, ALU.add))
                link(g.tensor_tensor(rqk[:, 1, :], rqk[:, 0, :], mhalf[:, :], ALU.pow))
                link(g.tensor_scalar(rqk[:, 1, 0:HEADS], rqk[:, 1, 0:HEADS], HD ** -0.5, None, ALU.mult))
                rs = rqk[:, 1, :].rearrange("p (h a) -> p h a", a=1).to_broadcast([P, NQK, HD])
                link(g.tensor_tensor(r, r, rs, ALU.mult))
                if i >= 2:
                    full(pool, ("kT", i - 2))
                out = rot[i % 2]
                qo = out[:, 0:HEADS * HD].rearrange("p (c a d) -> p a c d", c=PAIRS, a=2)
                ko = out[:, HEADS * HD:NQK * HD].rearrange("p (a c d) -> p a c d", a=2, c=1)
                for odd in range(2):
                    for n, tabx, h0, h1 in ((0, qtab, 0, HEADS), (1, ktab, HEADS, NQK)):
                        for m in range(2):
                            t = tabx[:, pos, 2 * odd + m:2 * odd + m + 1, :].to_broadcast([P, h1 - h0, 32])
                            last = g.tensor_tensor(rtmp[m][:, h0:h1, :], r[:, h0:h1, m:HD:2], t, ALU.mult)
                    link(last)
                    for a in range(2):
                        last = g.tensor_tensor(qo[:, a, :, odd:HD:2], rtmp[0][:, 4 * a:4 * a + 4, :],
                                               rtmp[1][:, 4 * a:4 * a + 4, :], ALU.add if odd else ALU.subtract)
                    last = g.tensor_tensor(ko[:, :, 0, odd:HD:2], rtmp[0][:, HEADS:NQK, :], rtmp[1][:, HEADS:NQK, :],
                                           ALU.add if odd else ALU.subtract)
                    if odd == 0:
                        link(last)
                last.then_inc(rot_ready, 1)

            def normalise(units, u0):
                for u in range(len(units)):
                    width = units[u][4]
                    pool.wait_ge(inv_ready, u0 + u + 1)
                    g.tensor_scalar(prob[u % 4][:, 0:width], prob[u % 4][:, 0:width], rinv[:, u % 4:u % 4 + 1],
                                    None, ALU.mult).then_inc(prob_ready, 1)

            normalise(SELF, 0)
            norms(sorted(LN_1 + LN_M))
            normalise(CROSS, len(SELF))

            norms(LN_2)

            for a, st in ((desc, (-1, EPG, EPG)), (eiota, (1, NE, 0)), (thr, (C, BLOCKS - 1, C)),
                          (bcol, (NE, BLOCKS - 1, NE - BLOCKS * NE))):
                g.iota(a, pattern=[[st[0], st[1]]], base=st[2], channel_multiplier=0,
                       allow_small_or_imprecise_dtypes=True).then_inc(route_const, 1)
            g.iota(jb, pattern=[[-1, BLOCKS - 1], [1, LIST]], base=0, channel_multiplier=0,
                   allow_small_or_imprecise_dtypes=True).then_inc(route_const, 1)
            g.iota(ecol[:, 0:1], pattern=[[0, 1]], base=0, channel_multiplier=1,
                   allow_small_or_imprecise_dtypes=True).then_inc(route_const, 1)
            pool.wait_ge(table_init, 16)
            for k in range(2):
                pool.wait_ge(slots_ready, k + 1)
                for i in range(NT):
                    g.indirect_dma_start(table_dram, bass.IndirectOffsetOnAxis(ap=slots[:, k, i:i + 1], axis=0),
                                         tvals[:, i, k, :], None, bounds_check=T * NE - 1,
                                         oob_is_err=False).then_inc(table_done, 16)

            last_token, last_pair = pool.to_reg(T - 1), pool.to_reg(2 * T - 1)

            def gather(j, b, col):
                if later(j - b):
                    pool.wait_ge(rowsT_full, j - NB + 1)
                g.tensor_copy(gidx[b][:, :], col[0]).then_inc(gidx_ready, 1)
                pool.wait_ge(gidx_ready, j + 1)
                pool.sem_inc(index_seen, 1)
                g.indirect_dma_start(xg[b], None, h2_dram, bass.IndirectOffsetOnAxis(ap=gidx[b][:, :], axis=0),
                                     bounds_check=last_token, oob_is_err=False).then_inc(rows_in[b], 16)

            def scatter(j, b, col, uses):
                if later(uses):
                    pool.wait_ge(rows_out[b], 16 * uses)
                g.tensor_copy(sidx[b][:, :], col[1]).then_inc(sidx_ready, 1)
                pool.wait_ge(sidx_ready, j + 1)
                pool.wait_ge(yo_a, j + 1)
                pool.wait_ge(yo_d, j + 1)
                pool.sem_inc(index_seen, 1)
                g.indirect_dma_start(pair_dram, bass.IndirectOffsetOnAxis(ap=sidx[b][:, :], axis=0), yo[b], None,
                                     bounds_check=last_pair, oob_is_err=False).then_inc(rows_out[b], 16)

            def col(c):
                return tab[:, bass.ds(2 * c, 1)], tab[:, bass.ds(2 * c + 1, 1)]

            pool.wait_ge(h2_stored, 16 * NT)
            pool.wait_ge(tab_in, 16)
            full(pool, ("co", NT - 1, 1))

            def quad(i):
                for b in range(NB):
                    j = NB * i + b
                    gather(j + AHEAD, (b + AHEAD) % NB, col(j + AHEAD))
                    scatter(j, b % 2, col(j), 2 * i + b // 2)

            for j in range(AHEAD):
                gather(j, j, col(j))
            quad(0)
            with pool.Fori(1, NE // NB - 1) as i:
                quad(i)
            pool.wait_ge(ctl_ready, 1)
            listed = [pool.value_load(ctl[0:1, 1 + LIST + b:2 + LIST + b], min_val=0, max_val=BLOCKS * NE)
                      for b in range(STEADY - NE)]
            cols = {j: col(j if j < NE else listed[j - NE]) for j in range(NE - NB, STEADY)}
            for j in range(NE - NB, STEADY):
                if j + AHEAD < STEADY:
                    gather(j + AHEAD, (j + AHEAD) % NB, cols[j + AHEAD])
                scatter(j, j % 2, cols[j], j // 2)
            for b in range(2):
                pool.wait_ge(rows_out[b], 16 * (STEADY // 2))
            n_over = pool.value_load(ctl[0:1, 0:1], min_val=0, max_val=LIST)
            with pool.Fori(1, PAIRS_OVER) as i:
                with pool.If(2 * i < n_over):
                    cs = [pool.value_load(ctl[0:1, bass.ds(1 + LIST + 2 * i + b, 1)], min_val=0,
                                          max_val=BLOCKS * NE) for b in range(2)]
                    for b in range(2):
                        gather(NE + 2 * i + b, b, col(cs[b]))
                    for b in range(2):
                        scatter(NE + 2 * i + b, b, col(cs[b]), NE // 2 + i)
                    for b in range(2):
                        pool.wait_ge(rows_out[b], 16 * (NE // 2 + 1 + i))
            pool.sem_inc(prow_used, 1)

            norms(LN_3)

        @block.scalar
        def _(act):
            a = nc.scalar

            def transposed_out(key, dst, n=4):
                bank = full(act, key)
                a.activation(dst, bank[:, 0:n * P].rearrange("p (k t) -> p k t", k=n), ACT.Copy)

            act.wait_ge(const_ready, 1)
            bank = full(act, "cpar")
            a.activation(cpar[:, :, :], bank[:, 0:CC * (TAPS + 3)].rearrange("p (c n) -> p c n", c=CC),
                         ACT.Copy).then_inc(free("cpar"), 1)

            def rows_T(layer, i):
                for j in range(2):
                    key = ("hT", layer, i, j)
                    bank = full(act, key)
                    dst = (catv if layer == 2 else hTv)[:, 4 * j:4 * j + 4, i * P:(i + 1) * P]
                    a.activation(dst, bank.rearrange("p (k t) -> p k t", k=4), ACT.Copy).then_inc(free(key), 1)

            for n in LN_X:
                act_hat(act, n)
                if n >= 1:
                    rows_T(0, n - 1)
            rows_T(0, NT - 1)

            for c in range(CC):
                for s, (t0, length) in enumerate(SEQS):
                    u0 = t0 + PAD + 2 * PAD * s
                    bank = full(act, ("a", c, s))
                    a.activation(upad[:, c, u0:u0 + length], bank[:, 0:length], ACT.Copy).then_inc(free(("a", c, s)), 1)
                    bank = full(act, ("g", c, s))
                    a.activation(sig[:, c, t0:t0 + length], bank[:, 0:length], ACT.Sigmoid).then_inc(free(("g", c, s)), 1)

            def qk_T(i):
                for key, dst, n in ((("qT", i), qT[:, :, i * P:(i + 1) * P], 4), (("kT", i), kT[:, i * P:(i + 1) * P], 1)):
                    bank = full(act, key)
                    src = bank.rearrange("p (k t) -> p k t", k=4) if n == 4 else bank[:, 0:P]
                    a.activation(dst, src, ACT.Copy).then_inc(free(key), 1)

            for i in range(NT):
                if i >= 2:
                    act.wait_ge(rot_ready, i - 1)
                r = raw[i % 2]
                bank = full(act, ("q", i))
                for h in range(HEADS):
                    a.activation(squares[i % 2][:, h * HD:(h + 1) * HD], bank[:, h * HD:(h + 1) * HD], ACT.Square,
                                 accum_out=ssq[:, i, h:h + 1])
                a.activation(r[:, 0:HEADS, :], bank.rearrange("p (h d) -> p h d", h=HEADS),
                             ACT.Copy).then_inc(free(("q", i)), 1)
                bank = full(act, ("kv", i))
                for h in range(KV_HEADS):
                    a.activation(squares[i % 2][:, (HEADS + h) * HD:(HEADS + h + 1) * HD],
                                 bank[:, h * HD:(h + 1) * HD], ACT.Square,
                                 accum_out=ssq[:, i, HEADS + h:HEADS + h + 1])
                a.activation(r[:, HEADS:NQK, :], bank[:, 0:P].rearrange("p (h d) -> p h d", h=KV_HEADS),
                             ACT.Copy).then_inc(qkv_raw, 1)
                a.activation(vtok[:, i, :], bank[:, P:2 * P], ACT.Copy).then_inc(free(("kv", i)), 1)
                if i >= 2:
                    qk_T(i - 2)
            for i in range(NT - 2, NT):
                qk_T(i)

            for s, (t0, length) in enumerate(SEQS):
                was_read(act, ("mean", s))
                a.activation(convsq[:, :, t0:t0 + length], acc[:, :, t0:t0 + length], ACT.Square).then_inc(conv_sq, 1)
            for s, (t0, length) in enumerate(SEQS):
                bank = full(act, ("var", s))
                a.activation(crstd[:, t0:t0 + length], bank[:, 0:length], ACT.Sqrt,
                             bias=epsv[:, 0:1]).then_inc(free(("var", s)), 1)
            for c in range(CC):
                act.wait_ge(conv_norm, c + 1)
                a.activation(acc[:, c, :], acc[:, c, :], ACT.Silu, bias=cpar[:, c, TAPS + 2:TAPS + 3],
                             scale=cpar[:, c, TAPS + 1:TAPS + 2]).then_inc(conv_out, 1)

            def exps(kind, units, u0):
                done = []

                def head_out(n):
                    s, h = next((s, h) for m, s, h, _, _ in units if m == n)
                    t0, length = SEQS[s]
                    if kind == "s":
                        key, half = ("sO", n, 0), h % 2 * HD
                        full(act, key)
                        b = place[key][0]
                        a.activation(catv[half:half + HD, h // 2, t0:t0 + length],
                                     ps[half:half + HD, b, 0:length], ACT.Copy).then_inc(free(key), 1)
                    else:
                        for j in range(2):
                            key = ("xO", n, j)
                            bank = full(act, key)
                            a.activation(hTv[:, 2 * h + j, t0:t0 + length], bank[:, 0:length],
                                         ACT.Copy).then_inc(free(key), 1)

                for u, (n, s, h, i, width) in enumerate(units):
                    last = u - S_AHEAD - 2
                    if last >= 0 and units[last][0] != units[last + 1][0]:
                        head_out(units[last][0])
                        done.append(units[last][0])
                    act.wait_ge(max_ready, u0 + u + 1)
                    if u >= 4:
                        full(act, (kind + "T", u - 4))
                    key = (kind + "S", u)
                    a.activation(prob[u % 4][:, 0:width], ps[:, place[key][0], 0:width], ACT.Exp,
                                 bias=nmax[:, u % 4:u % 4 + 1],
                                 accum_out=rsum[:, u % 4:u % 4 + 1]).then_inc(free(key), 1)
                for n in range(units[-1][0] + 1):
                    if n not in done:
                        head_out(n)

            exps("s", SELF, 0)

            def mem_T(i):
                for j in range(2):
                    key = ("mT", i, j)
                    bank = full(act, key)
                    a.activation(mT[:, 4 * j:4 * j + 4, i * P:(i + 1) * P], bank.rearrange("p (k t) -> p k t", k=4),
                                 ACT.Copy).then_inc(free(key), 1)

            for n in sorted(LN_1 + LN_M[0:2]):
                act_hat(act, n)
            for i in range(2):
                mem_T(i)
            rows_T(1, 0)
            rows_T(1, 1)
            act_hat(act, LN_M[2])
            rows_T(1, 2)
            act_hat(act, LN_M[3])
            rows_T(1, 3)
            for i in range(2, MT):
                mem_T(i)
            for c in range(KC):
                bank = full(act, ("ck", c))
                a.activation(kmT[:, c, :], bank, ACT.Copy).then_inc(free(("ck", c)), 1)
            for i in range(MT):
                for j in range(2):
                    bank = full(act, ("cv", i, j))
                    a.activation(vm[:, i, 512 * j:512 * (j + 1)], bank, ACT.Copy).then_inc(free(("cv", i, j)), 1)
            for i in range(MT, NT):
                rows_T(1, i)
            for c in range(KC):
                for s, (t0, length) in enumerate(SEQS):
                    bank = full(act, ("cq", c, s))
                    a.activation(catv[:, c, t0:t0 + length], bank[:, 0:length], ACT.Copy,
                                 scale=MHD ** -0.5).then_inc(free(("cq", c, s)), 1)
            exps("x", CROSS, len(SELF))
            for k, n in enumerate(LN_2):
                act_hat(act, n)
                if k >= 1:
                    rows_T(2, k - 1)
            rows_T(2, NT - 1)

            act.wait_ge(h2_stored, 16 * NT)
            for i in range(NT):
                was_read(act, ("hT", 2, i, 1))
                a.activation(hres[:, i, :], hres[:, i, :], ACT.Copy, scale=ALPHA).then_inc(scaled, 1)
            act.wait_ge(route_dve, 1)
            a.activation(gex, gex, ACT.Exp).then_inc(route_exp, 1)
            act.wait_ge(route_dve, 2)
            a.activation(ev, ev, ACT.Exp).then_inc(route_exp, 1)

            def block_act_T(j, b):
                act.wait_ge(rowsT_full, j + 1)
                a.activation(xT[b][:, 0:4, :], ps[:, 4, :].rearrange("p (k t) -> p k t", k=4),
                             ACT.Copy).then_inc(rowsT_a, 1)

            def block_act(j, b, uses):
                act.wait_ge(gu_full, j + 1)
                if later(uses):
                    act.wait_ge(hid_ready, j - 1)
                a.activation(act_g[b], ps[:, b, 0:256].rearrange("p (k t) -> p k t", k=2),
                             ACT.Silu).then_inc(silu_done, 1)

            def block_act_out(j, b, uses):
                act.wait_ge(down_full, j + 1)
                if later(uses):
                    act.wait_ge(rows_out[b], 16 * uses)
                a.activation(yo[b][:, 0:512], ps[:, 2 + 4 * b, :], ACT.Copy).then_inc(yo_a, 1)

            def blocks(j0, n, half, end=False):
                for b in range(n):
                    block_act(j0 + b, b % 2, half + b // 2)
                    if not (end and b == n - 1):
                        block_act_T(j0 + b + 1, (b + 1) % 2)
                    block_act_out(j0 + b, b % 2, half + b // 2)

            block_act_T(0, 0)
            blocks(0, NB, 0)
            with act.Fori(1, NE // NB - 1) as i:
                blocks(NB * i, NB, 2 * i)
            blocks(NE - NB, NB + STEADY - NE, (NE - NB) // 2, end=True)
            act.wait_ge(ctl_ready, 1)
            n_over = act.value_load(ctl[0:1, 0:1], min_val=0, max_val=LIST)
            with act.Fori(1, PAIRS_OVER) as i:
                with act.If(2 * i < n_over):
                    for b in range(2):
                        block_act_T(NE + 2 * i + b, b)
                        block_act(NE + 2 * i + b, b, NE // 2 + i)
                        block_act_out(NE + 2 * i + b, b, NE // 2 + i)
            for n in LN_3:
                act_hat(act, n)

        @block.vector
        def _(dve):
            v = nc.vector
            steps = [0]

            def link(ins):
                steps[0] += 1
                ins.then_inc(dve_step, 1)
                dve.wait_ge(dve_step, steps[0])

            for n in LN_X:
                dve.wait_ge(x_in[n], 16)
                dve_stats(dve, n, link)
                if n >= 2:
                    dve_bias(dve, n - 2)
            for n in LN_X[-2:]:
                dve_bias(dve, n)

            conv = [0]
            for c in range(CC):
                was_read(dve, ("g", c, 1))
                was_read(dve, ("a", c, 1))
                was_read(dve, ("g", c, 0))
                for s, (t0, length) in enumerate(SEQS):
                    u0 = t0 + PAD + 2 * PAD * s
                    last = v.tensor_tensor(upad[:, c, u0:u0 + length], upad[:, c, u0:u0 + length],
                                           sig[:, c, t0:t0 + length], ALU.mult)
                link(last)
                if c == 0:
                    was_read(dve, "cpar")
                for k in range(TAPS):
                    for s, (t0, length) in enumerate(SEQS):
                        u0 = t0 + 2 * PAD * s + k
                        src, dst = upad[:, c, u0:u0 + length], acc[:, c, t0:t0 + length]
                        if k == 0:
                            ins = v.tensor_scalar(dst, src, cpar[:, c, 0:1], cpar[:, c, TAPS:TAPS + 1], ALU.mult, ALU.add)
                        else:
                            dve.wait_ge(conv_done, conv[0] - 1)
                            ins = v.scalar_tensor_tensor(out=dst, in0=src, scalar=cpar[:, c, k:k + 1], in1=dst,
                                                         op0=ALU.mult, op1=ALU.add)
                        ins.then_inc(conv_done, 1)
                        conv[0] += 1
            dve.wait_ge(conv_done, conv[0])
            mean = [full(dve, ("mean", s)) for s in range(2)]
            for s, (t0, length) in enumerate(SEQS):
                for c in range(CC):
                    last = v.tensor_tensor(acc[:, c, t0:t0 + length], acc[:, c, t0:t0 + length], mean[s][:, 0:length],
                                           ALU.subtract)
                last.then_inc(free(("mean", s)), 1)
            for s, (t0, length) in enumerate(SEQS):
                was_read(dve, ("var", s))
            link(v.reciprocal(crstd, crstd))
            for c in range(CC):
                v.tensor_tensor(acc[:, c, :], acc[:, c, :], crstd, ALU.mult).then_inc(conv_norm, 1)

            def softmax(kind, units, u0):
                wide = 4 if kind == "s" else 2

                def inverse(u):
                    was_read(dve, (kind + "S", u))
                    v.reciprocal(rinv[:, u % 4:u % 4 + 1], rsum[:, u % 4:u % 4 + 1]).then_inc(inv_ready, 1)

                def turned(u):
                    n, s, h, i, width = units[u]
                    key = (kind + "T", u)
                    bank = full(dve, key)
                    if n >= 2:
                        full(dve, (kind + "O", n - 2, 0 if kind == "s" else 1))
                    m = width // P
                    v.tensor_copy(PT[n % 2][:, 0:m, i * P:(i + 1) * P],
                                  bank[:, 0:width].rearrange("p (k t) -> p k t", k=m)).then_inc(free(key), 1)

                for u, (n, s, h, i, width) in enumerate(units):
                    bank = full(dve, (kind + "S", u))
                    if u >= 4:
                        was_read(dve, (kind + "S", u - 4))
                    v.tensor_reduce(nmax[:, u % 4:u % 4 + 1], bank[:, 0:width], AX.X, ALU.max,
                                    negate=True).then_inc(max_ready, 1)
                    if u >= 1:
                        inverse(u - 1)
                    if u >= S_AHEAD:
                        turned(u - S_AHEAD)
                inverse(len(units) - 1)
                for u in range(len(units) - S_AHEAD, len(units)):
                    turned(u)

            softmax("s", SELF, 0)

            def residual(key, i, j):
                bank = full(dve, key)
                rows = hres[:, i, 512 * j:512 * (j + 1)]
                return v.scalar_tensor_tensor(out=rows, in0=rows, scalar=ALPHA, in1=bank, op0=ALU.mult, op1=ALU.add)

            order = sorted(LN_1 + LN_M)
            seen = 0
            for k, n in enumerate(order):
                if n in LN_1:
                    i = LN_1.index(n)
                    for j in range(2):
                        residual(("mix", i, j), i, j).then_inc(free(("mix", i, j)), 1)
                        was_read(dve, ("mix", i, j))
                        seen += 1
                else:
                    i = LN_M.index(n)
                    dve.wait_ge(mem_in[i % 2], 16 * (i // 2 + 1))
                dve_stats(dve, n, link)
                if k >= 2:
                    dve_bias(dve, order[k - 2])
            for n in order[-2:]:
                dve_bias(dve, n)
            softmax("x", CROSS, len(SELF))
            for k, n in enumerate(LN_2):
                for j in range(2):
                    residual(("co", k, j), k, j).then_inc(free(("co", k, j)), 1)
                    was_read(dve, ("co", k, j))
                dve_stats(dve, n, link)
                if k >= 2:
                    dve_bias(dve, LN_2[k - 2])
            for n in LN_2[-2:]:
                dve_bias(dve, n)

            dve.wait_ge(small_in, 32)
            bank = full(dve, "route")
            v.tensor_tensor(lg, bank[:, 0:NT * NR].rearrange("p (t n) -> p t n", t=NT),
                            br.rearrange("p (a n) -> p a n", a=1).to_broadcast([P, NT, NR]),
                            ALU.add).then_inc(free("route"), 1)
            was_read(dve, "route")
            dve.wait_ge(route_const, 6)

            def over(a, n):
                return a.rearrange("p (t a) -> p t a", a=1).to_broadcast([P, NT, n])

            def along(a, n):
                return a.rearrange("p (a e) -> p a e", a=1).to_broadcast([P, NT, n])

            def first_max(vals, n, top, mask, tmp, out):
                link(v.tensor_reduce(top, vals, AX.X, ALU.max))
                link(v.tensor_tensor(mask, vals, over(top, n), ALU.is_equal))
                link(v.tensor_tensor(mask, mask, along(desc[:, EPG - n:EPG], n), ALU.mult))
                link(v.tensor_reduce(tmp, mask, AX.X, ALU.max))
                link(v.tensor_tensor(out, mask, over(tmp, n), ALU.is_equal))

            gl, el = lg[:, :, 0:GROUPS], lg[:, :, GROUPS:NR]
            first_max(gl, GROUPS, gmx, geq, gm2, G)
            v.tensor_tensor(gex, gl, over(gmx, GROUPS), ALU.subtract).then_inc(route_dve, 1)
            for g_ in range(GROUPS):
                last = v.tensor_tensor(esel4[:, :, g_, :], el[:, :, EPG * g_:EPG * (g_ + 1)],
                                       G[:, :, g_:g_ + 1].to_broadcast([P, NT, EPG]), ALU.mult)
            link(last)
            link(v.tensor_reduce(esel, esel4.rearrange("p t g e -> p t e g"), AX.X, ALU.add))
            first_max(esel, EPG, v1, eq, m1, H1)
            link(v.scalar_tensor_tensor(out=e2, in0=H1, scalar=-3.0e38, in1=esel, op0=ALU.mult, op1=ALU.add))
            first_max(e2, EPG, v2, eq, m2, H2)
            v.tensor_tensor(ev, v2, v1, ALU.subtract).then_inc(route_dve, 1)
            for k, H in enumerate((H1, H2)):
                for g_ in range(GROUPS):
                    last = v.tensor_tensor(pick[k][:, :, g_, :], H, G[:, :, g_:g_ + 1].to_broadcast([P, NT, EPG]), ALU.mult)
            link(last)
            pk = [q.rearrange("p t g e -> p t (g e)") for q in pick]
            v.tensor_tensor(both, pk[0], pk[1], ALU.add).then_inc(route_dve, 1)
            bank = full(dve, "rank")
            link(v.scalar_tensor_tensor(out=rk, in0=bank[:, 0:NT * NE].rearrange("p (t e) -> p t e", t=NT),
                                        scalar=float(NE), in1=along(eiota, NE), op0=ALU.mult, op1=ALU.add))
            for k in range(2):
                link(v.tensor_tensor(rkp, rk, pk[k], ALU.mult))
                link(v.tensor_reduce(slotf, rkp, AX.X, ALU.add))
                v.tensor_copy(slots[:, k, :], slotf).then_inc(slots_ready, 1)
                dve.wait_ge(slots_ready, k + 1)
            dve.wait_ge(route_exp, 2)
            link(v.tensor_reduce(gsum, gex, AX.X, ALU.add))
            link(v.reciprocal(pgrp, gsum))
            link(v.tensor_scalar(den, ev, 1.0, None, ALU.add))
            link(v.reciprocal(den, den))
            link(v.tensor_tensor(pw[:, 0, :], pgrp, den, ALU.mult))
            link(v.tensor_tensor(pw[:, 1, :], pw[:, 0, :], ev, ALU.mult))
            bank = full(dve, "count")
            link(v.tensor_copy(cnt[0:NE], bank[0:NE, 0:1]))
            link(v.tensor_scalar(more[0:NE], thr[0:NE], cnt[0:NE], None, ALU.is_lt))
            v.tensor_reduce(cnt[0:NE], more[0:NE], AX.X, ALU.add).then_inc(counts_in, 1)
            bank = full(dve, "base")
            link(v.tensor_copy(base[0:NE], bank[0:NE, 0:1]))
            link(v.tensor_scalar(hitm[0:NE], jb[0:NE], base[0:NE], None, ALU.is_equal))
            v.tensor_tensor(hitm[0:NE], hitm[0:NE],
                            more[0:NE].rearrange("p (b a) -> p b a", a=1).to_broadcast([NE, BLOCKS - 1, LIST]),
                            ALU.mult).then_inc(counts_in, 1)
            bank = full(dve, "list")
            w = (BLOCKS - 1) * LIST
            link(v.tensor_copy(lst[0:1], bank[0:1, 0:2 * w]))
            le = lst[0:1, 0:w].rearrange("p (b j) -> p j b", j=LIST)
            l1 = lst[0:1, w:2 * w].rearrange("p (b j) -> p b j", j=LIST)
            link(v.tensor_tensor(lstb[0:1].rearrange("p (b j) -> p b j", j=LIST), l1,
                                 bcol[0:1].rearrange("p (b a) -> p b a", a=1).to_broadcast([1, BLOCKS - 1, LIST]),
                                 ALU.mult))
            link(v.tensor_reduce(res[0:1, 0:1], lst[0:1, w:2 * w], AX.X, ALU.add))
            link(v.tensor_reduce(res[0:1, 1:1 + LIST], le, AX.X, ALU.add))
            link(v.tensor_reduce(res[0:1, 1 + LIST:1 + 2 * LIST], lstb[0:1].rearrange("p (b j) -> p j b", j=LIST),
                                 AX.X, ALU.add))
            link(v.scalar_tensor_tensor(out=res[0:1, 1 + LIST:1 + 2 * LIST], in0=res[0:1, 1 + LIST:1 + 2 * LIST],
                                        scalar=float(BLOCKS * NE), in1=res[0:1, 1:1 + LIST], op0=ALU.add, op1=ALU.add))
            v.tensor_copy(ctl[:, :], res[0:1, :]).then_inc(ctl_ready, 1)

            def block_dve_T(j, b):
                dve.wait_ge(rowsT_full, j + 1)
                v.tensor_copy(xT[b][:, 4:8, :], ps[:, 5, :].rearrange("p (k t) -> p k t", k=4)).then_inc(rowsT_d, 1)

            def block_dve(j, b, uses):
                if later(uses):
                    dve.wait_ge(down_full, j - 1)
                dve.wait_ge(silu_done, j + 1)
                v.tensor_tensor(hid[b], act_g[b], ps[:, b, 256:512].rearrange("p (k t) -> p k t", k=2),
                                ALU.mult).then_inc(hid_ready, 1)

            def block_dve_out(j, b, uses):
                dve.wait_ge(down_full, j + 1)
                if later(uses):
                    dve.wait_ge(rows_out[b], 16 * uses)
                v.tensor_copy(yo[b][:, 512:1024], ps[:, 3 + 4 * b, :]).then_inc(yo_d, 1)

            def blocks(j0, n, half, end=False):
                for b in range(n):
                    block_dve(j0 + b, b % 2, half + b // 2)
                    if not (end and b == n - 1):
                        block_dve_T(j0 + b + 1, (b + 1) % 2)
                    block_dve_out(j0 + b, b % 2, half + b // 2)

            block_dve_T(0, 0)
            blocks(0, NB, 0)
            with dve.Fori(1, NE // NB - 1) as i:
                blocks(NB * i, NB, 2 * i)
            blocks(NE - NB, NB + STEADY - NE, (NE - NB) // 2, end=True)
            dve.wait_ge(ctl_ready, 1)
            n_over = dve.value_load(ctl[0:1, 0:1], min_val=0, max_val=LIST)
            with dve.Fori(1, PAIRS_OVER) as i:
                with dve.If(2 * i < n_over):
                    for b in range(2):
                        block_dve_T(NE + 2 * i + b, b)
                        block_dve(NE + 2 * i + b, b, NE // 2 + i)
                        block_dve_out(NE + 2 * i + b, b, NE // 2 + i)

            for k, n in enumerate(LN_3):
                rows = hres[:, k, :]
                if k >= 2:
                    dve_bias(dve, LN_3[k - 2])
                dve.wait_ge(scaled, NT)
                for c in range(2):
                    dve.wait_ge(prow_in[2 * (k % 3) + c], 16 * (k // 3 + 1))
                    link(v.scalar_tensor_tensor(out=rows, in0=prow[2 * (k % 3) + c], scalar=pw[:, c, k:k + 1], in1=rows,
                                                op0=ALU.mult, op1=ALU.add))
                dve_stats(dve, n, link)
            for n in LN_3[-2:]:
                dve_bias(dve, n)

        @block.tensor
        def _(pe):
            t = nc.tensor

            def claim(key):
                b, n = place[key]
                if n:
                    pe.wait_ge(bank_free[b], n)
                return ps[:, b, :]

            def done(key, last):
                last.then_inc(bank_full[place[key][0]], 1)

            def slab(name):
                n = slab_names.index(name)
                pe.wait_ge(slab_in[n % 3], 16 * (n // 3 + 1))
                w = w_slabs[n][1].shape[1]
                return ring[:, n % 3, 0:KC * w].rearrange("p (k c) -> p k c", k=KC)

            def product(key, out_of, lhs, rhs):
                bank = claim(key)
                for k in range(KC):
                    last = t.matmul(out_of(bank), lhs(k), rhs(k), start=(k == 0), stop=(k == KC - 1))
                return last

            def rows_T(layer, i, rows, n):
                pe.wait_ge(ln_done, n + 1)
                for j in range(2):
                    key = ("mT", i, j) if layer == "m" else ("hT", layer, i, j)
                    bank = claim(key)
                    for c in range(4):
                        last = t.transpose(bank[:, c * P:(c + 1) * P], rows[:, (4 * j + c) * P:(4 * j + c + 1) * P],
                                           ident[:, :])
                    done(key, last)

            pe.wait_ge(const_ready, 1)
            pe.wait_ge(conv_in, 16)
            bank = claim("cpar")
            for c in range(CC):
                last = t.transpose(bank[:, c * (TAPS + 3):(c + 1) * (TAPS + 3)], cpar_in[:, c * P:(c + 1) * P],
                                   ident[0:TAPS + 3, 0:TAPS + 3])
            done("cpar", last)
            for i in range(NT):
                rows_T(0, i, hres[:, i, :], LN_X[i])
            for i in (NT - 1,):
                for j in range(2):
                    was_read(pe, ("hT", 0, i, j))
            wa, wg = slab("a"), slab("g")
            for c in range(CC):
                for s, (t0, length) in enumerate(SEQS):
                    for name, w in (("a", wa), ("g", wg)):
                        last = product((name, c, s), lambda k: k[:, 0:length], lambda k: w[:, k, c * P:(c + 1) * P],
                                       lambda k: hTv[:, k, t0:t0 + length])
                        done((name, c, s), last)
            def qk_T(i):
                pe.wait_ge(rot_ready, i + 1)
                bank = claim(("qT", i))
                for c in range(PAIRS):
                    last = t.transpose(bank[:, c * P:(c + 1) * P], rot[i % 2][:, c * P:(c + 1) * P], ident[:, :])
                done(("qT", i), last)
                bank = claim(("kT", i))
                last = t.transpose(bank[:, 0:P], rot[i % 2][:, PAIRS * P:(PAIRS + 1) * P], ident[:, :])
                done(("kT", i), last)

            wq, wkv = slab("q"), slab("kv")
            for i in range(NT):
                for name, w, n in (("q", wq, 512), ("kv", wkv, 256)):
                    last = product((name, i), lambda k: k[:, 0:n], lambda k: hTv[:, k, i * P:(i + 1) * P],
                                   lambda k: w[:, k, :])
                    done((name, i), last)
                if i >= 2:
                    qk_T(i - 2)
            for i in range(NT - 2, NT):
                qk_T(i)

            pe.wait_ge(conv_done, 2 * CC * TAPS)
            for what in ("mean", "var"):
                for s, (t0, length) in enumerate(SEQS):
                    bank = claim((what, s))
                    for c in range(CC):
                        if what == "var" and c == 0:
                            pe.wait_ge(conv_sq, s + 1)
                        last = t.matmul(bank[:, 0:length], ones_c[:, :],
                                        (acc if what == "mean" else convsq)[:, c, t0:t0 + length],
                                        start=(c == 0), stop=(c == CC - 1))
                    done((what, s), last)

            def attention(kind, units, u0, n0):
                def scores(u):
                    n, s, h, i, width = units[u]
                    bank = claim((kind + "S", u))
                    t0 = SEQS[s][0] + i * P
                    if kind == "s":
                        half = h // PAIRS * HD
                        last = t.matmul(bank[:, 0:width], qT[half:half + HD, h % PAIRS, t0:t0 + P],
                                        kT[half:half + HD, SEQS[s][0]:SEQS[s][0] + width], start=True, stop=True)
                    else:
                        for j in range(2):
                            last = t.matmul(bank[:, 0:width], catv[:, 2 * h + j, t0:t0 + P],
                                            kmT[:, 2 * h + j, s * N_MEM:(s + 1) * N_MEM], start=(j == 0), stop=(j == 1))
                    done((kind + "S", u), last)

                def turn(u):
                    width = units[u][4]
                    bank = claim((kind + "T", u))
                    pe.wait_ge(prob_ready, u0 + u + 1)
                    for k in range(width // P):
                        last = t.transpose(bank[:, k * P:(k + 1) * P], prob[u % 4][:, k * P:(k + 1) * P], ident[:, :])
                    done((kind + "T", u), last)

                def values(n):
                    us = [u for u in range(len(units)) if units[u][0] == n]
                    _, s, h, _, width = units[us[0]]
                    length = SEQS[s][1]
                    for u in us[-2:]:
                        was_read(pe, (kind + "T", u))
                    for j in range(1 if kind == "s" else 2):
                        key = (kind + "O", n, j)
                        claim(key)
                        b = place[key][0]
                        for k in range(width // P):
                            if kind == "s":
                                half = h % 2 * HD
                                out = ps[half:half + HD, b, 0:length]
                                lhs = vtok[:, SEQS[s][0] // P + k, h // PAIRS * HD:(h // PAIRS + 1) * HD]
                            else:
                                out = ps[:, b, 0:length]
                                lhs = vm[:, s * N_MEM // P + k, h * MHD + j * P:h * MHD + (j + 1) * P]
                            last = t.matmul(out, lhs, PT[n % 2][:, k, 0:length], start=(k == 0),
                                            stop=(k == width // P - 1))
                        done(key, last)

                pending = []
                for u in range(len(units) + S_AHEAD):
                    if u < len(units):
                        scores(u)
                    if u >= S_AHEAD:
                        turn(u - S_AHEAD)
                    for n in pending:
                        values(n)
                    pending = []
                    k = u - S_AHEAD
                    if k >= 0 and (k + 1 == len(units) or units[k + 1][0] != units[k][0]):
                        pending.append(units[k][0])
                for n in pending:
                    values(n)

            was_read(pe, ("qT", NT - 1))
            was_read(pe, ("kT", NT - 1))
            was_read(pe, ("kv", NT - 1))
            attention("s", SELF, 0, 0)

            wm = [slab("mix0"), slab("mix1")]
            pe.wait_ge(conv_out, CC)
            for n in range(SELF[-1][0] + 1)[-2:]:
                was_read(pe, ("sO", n, 0))
            for i in range(NT):
                for j in range(2):
                    last = product(("mix", i, j), lambda k: k, lambda k: catv[:, k, i * P:(i + 1) * P],
                                   lambda k: wm[j][:, k, :])
                    done(("mix", i, j), last)

            for i in range(2):
                rows_T("m", i, mrow[i % 2], LN_M[i])
            for i in range(MT):
                rows_T(1, i, hres[:, i, :], LN_1[i])
            for i in range(2, MT):
                rows_T("m", i, mrow[i % 2], LN_M[i])
            for j in range(2):
                was_read(pe, ("mT", MT - 1, j))
            for c in range(KC):
                w = slab(f"ck{c // 4}")
                last = product(("ck", c), lambda k: k, lambda k: w[:, k, c % 4 * P:(c % 4 + 1) * P], lambda k: mT[:, k, :])
                done(("ck", c), last)
            wv = [slab("cv0"), slab("cv1")]
            for i in range(MT):
                for j in range(2):
                    last = product(("cv", i, j), lambda k: k, lambda k: mT[:, k, i * P:(i + 1) * P],
                                   lambda k: wv[j][:, k, :])
                    done(("cv", i, j), last)
            for i in range(MT, NT):
                rows_T(1, i, hres[:, i, :], LN_1[i])
            for j in range(2):
                was_read(pe, ("hT", 1, NT - 1, j))
            for c in range(KC):
                w = slab(f"cq{c // 4}")
                for s, (t0, length) in enumerate(SEQS):
                    last = product(("cq", c, s), lambda k: k[:, 0:length], lambda k: w[:, k, c % 4 * P:(c % 4 + 1) * P],
                                   lambda k: hTv[:, k, t0:t0 + length])
                    done(("cq", c, s), last)
            for s in range(2):
                was_read(pe, ("cq", KC - 1, s))
            attention("x", CROSS, len(SELF), SELF[-1][0] + 1)
            wo = [slab("co0"), slab("co1")]
            for j in range(2):
                was_read(pe, ("xO", CROSS[-1][0], j))
            for i in range(NT):
                for j in range(2):
                    last = product(("co", i, j), lambda k: k, lambda k: hTv[:, k, i * P:(i + 1) * P],
                                   lambda k: wo[j][:, k, :])
                    done(("co", i, j), last)
            pe.wait_ge(small_in, 32)
            logits = claim("route")
            for i in range(NT):
                rows_T(2, i, hres[:, i, :], LN_2[i])
                for j in range(2):
                    was_read(pe, ("hT", 2, i, j))
                for k in range(KC):
                    last = t.matmul(logits[:, i * NR:(i + 1) * NR], catv[:, k, i * P:(i + 1) * P], wr[:, k, :],
                                    start=(k == 0), stop=(k == KC - 1))
            done("route", last)

            pe.wait_ge(route_dve, 3)
            bank = claim("rank")
            for i in range(NT):
                for m in range(i + 1):
                    last = t.matmul(bank[:, i * NE:(i + 1) * NE], (before if m == i else ones)[:, :], both[:, m, :],
                                    start=(m == 0), stop=(m == i))
            done("rank", last)
            bank = claim("count")
            for i in range(NT):
                last = t.matmul(bank[0:NE, 0:1], both[:, i, :], ones[:, 0:1], start=(i == 0), stop=(i == NT - 1))
            done("count", last)
            pe.wait_ge(counts_in, 1)
            bank = claim("base")
            last = t.matmul(bank[0:NE, 0:1], before[0:NE, 0:NE], cnt[0:NE], start=True, stop=True)
            done("base", last)
            pe.wait_ge(counts_in, 2)
            bank = claim("list")
            w = (BLOCKS - 1) * LIST
            hits = hitm[0:NE].rearrange("p b j -> p (b j)")
            t.matmul(bank[0:1, 0:w], ecol[0:NE, 0:1], hits, start=True, stop=True)
            last = t.matmul(bank[0:1, w:2 * w], ones[0:NE, 0:1], hits, start=True, stop=True)
            done("list", last)

            def block_T(j, b, r, uses):
                pe.wait_ge(rows_in[r], 16 * (uses + 1))
                if later(j):
                    pe.wait_ge(rowsT_a, j)
                    pe.wait_ge(rowsT_d, j)
                for c in range(KC):
                    last = t.transpose(ps[:, 4 + c // 4, c % 4 * P:(c % 4 + 1) * P], xg[r][:, c:D:KC],
                                       ident[:, :])
                last.then_inc(rowsT_full, 1)

            def block_gu(j, b, r, uses, half):
                pe.wait_ge(rowsT_a, j + 1)
                pe.wait_ge(rowsT_d, j + 1)
                pe.wait_ge(wexp_in[r], 48 * (uses + 1))
                if later(half):
                    pe.wait_ge(hid_ready, j - 1)
                for m, off in ((0, 0), (1, 2048)):
                    w = wexp[r][:, off:off + 2048].rearrange("p (k f) -> p k f", k=KC)
                    for f in range(2):
                        for k in range(KC):
                            last = t.matmul(ps[:, b, (2 * m + f) * P:(2 * m + f + 1) * P], w[:, k, f:FE:2],
                                            xT[b][:, k, :], start=(k == 0), stop=(k == KC - 1))
                last.then_inc(gu_full, 1)

            def block_down(j, b, r, half):
                pe.wait_ge(hid_ready, j + 1)
                if later(half):
                    pe.wait_ge(yo_a, j - 1)
                    pe.wait_ge(yo_d, j - 1)
                w = wexp[r][:, 4096:6144].rearrange("p (k f) -> p k f", k=2)
                for n in range(2):
                    for k in range(2):
                        last = t.matmul(ps[:, 2 + n + 4 * b, :], hid[b][:, k, :], w[:, k, n * 512:(n + 1) * 512],
                                        start=(k == 0), stop=(k == 1))
                last.then_inc(down_full, 1)

            def blocks(j0, n, q, half, end=False):
                for b in range(n):
                    block_gu(j0 + b, b % 2, b % NB, q + b // NB, half + b // 2)
                    if not (end and b == n - 1):
                        block_T(j0 + b + 1, (b + 1) % 2, (b + 1) % NB, q + (b + 1) // NB)
                    block_down(j0 + b, b % 2, b % NB, half + b // 2)

            block_T(0, 0, 0, 0)
            blocks(0, NB, 0, 0)
            with pe.Fori(1, NE // NB - 1) as i:
                blocks(NB * i, NB, i, 2 * i)
            blocks(NE - NB, NB + STEADY - NE, NE // NB - 1, (NE - NB) // 2, end=True)
            pe.wait_ge(ctl_ready, 1)
            n_over = pe.value_load(ctl[0:1, 0:1], min_val=0, max_val=LIST)
            with pe.Fori(1, PAIRS_OVER) as i:
                with pe.If(2 * i < n_over):
                    for b in range(2):
                        block_T(NE + 2 * i + b, b, b, NE // NB + i)
                        block_gu(NE + 2 * i + b, b, b, NE // NB + i, NE // 2 + i)
                        block_down(NE + 2 * i + b, b, b, NE // 2 + i)


def rope_tables():
    import numpy as np

    n = max(length for _, length in SEQS)
    t = np.arange(n)
    freq = (np.float32(10000.0) ** (-np.arange(0, 32, 2, dtype=np.float32) / np.float32(32))).astype(np.float32)
    ang = np.concatenate([(t // 64).astype(np.float32)[:, None] * freq,
                          (t % 64).astype(np.float32)[:, None] * freq], -1)
    return np.cos(ang).astype(np.float32), np.sin(ang).astype(np.float32)


def kernel(**inputs):
    import numpy as np
    import concourse.bacc as bacc
    from concourse.bass_utils import run_bass_kernel_spmd

    a = {k: np.asarray(v) for k, v in inputs.items()}
    cos, sin = rope_tables()
    arrays = {
        "x": np.concatenate([a["x_prompt"][0], a["x_sample"][0]]),
        "mem": np.concatenate([a["mem_prompt"][0], a["mem_sample"][0]]),
        "lnp": np.stack([a["ln_in_g"], a["ln_in_b"], a["ln1_g"][0], a["ln1_b"][0], a["ln2_g"][0], a["ln2_b"][0],
                         a["ln3_g"][0], a["ln3_b"][0], a["ln_mem_g"], a["ln_mem_b"]]),
        "rope_cos": cos, "rope_sin": sin, "q_gain": a["q_norm_g"][0], "k_gain": a["k_norm_g"][0],
        "conv_rows": np.concatenate([a["conv_w"][0], a["conv_b"], a["conv_ln_g"], a["conv_ln_b"]]),
        "w_router": np.concatenate([a["w_router_g"][0], a["w_router_e"][0].transpose(1, 0, 2).reshape(D, NE)], 1)
        .reshape(KC, P, NR).transpose(1, 0, 2),
        "b_router": np.concatenate([a["b_router_g"][0], a["b_router_e"][0].reshape(NE)]),
        "w_gate": a["w_e_gate"][0], "w_up": a["w_e_up"][0], "w_down": a["w_e_down"][0],
    }
    for name in ("w_in", "w_mix_out", "w_cq", "w_ck", "w_cv", "w_co"):
        arrays[name] = a[name][0]
    arrays = {k: np.ascontiguousarray(v) for k, v in arrays.items()}
    nc = bacc.Bacc("TRN2", target_bir_lowering=False, num_devices=1)
    d = {k: nc.dram_tensor(k, v.shape, mybir.dt.from_np(v.dtype), kind="ExternalInput").ap() for k, v in arrays.items()}
    y = nc.dram_tensor("y", (T, D), F32, kind="ExternalOutput").ap()
    slabs = weight_slabs(d["w_in"], d["w_mix_out"], d["w_ck"], d["w_cv"], d["w_cq"], d["w_co"])
    lnp = [d["lnp"][n] for n in range(10)]
    encoder(nc, d["x"], d["mem"], slabs, lnp, d["rope_cos"], d["rope_sin"], d["q_gain"], d["k_gain"], d["conv_rows"],
            d["w_router"], d["b_router"], d["w_gate"], d["w_up"], d["w_down"], y)
    r = run_bass_kernel_spmd(nc, [arrays], core_ids=[0])
    out = r.results[0]["y"]
    return out[0:256].reshape(1, 256, D), out[256:768].reshape(1, 512, D)
```

```python
from contextlib import ExitStack

import concourse.bass as bass
from concourse import mybir

F32 = mybir.dt.float32
I32 = mybir.dt.int32
U32 = mybir.dt.uint32
ALU = mybir.AluOpType
ACT = mybir.ActivationFunctionType
AX = mybir.AxisListType

P = 128
D = 1024
KC = D // P
SEQS = ((0, 256), (256, 512))
T = sum(n for _, n in SEQS)
NT = T // P
TILES = [(s, i) for s, (t0, n) in enumerate(SEQS) for i in range(t0 // P, (t0 + n) // P)]
HEADS, KV_HEADS, HD = 8, 2, 64
PAIRS = HEADS // KV_HEADS
NQK = HEADS + KV_HEADS
CONV, TAPS = 512, 31
PAD = TAPS // 2
CC = CONV // P
UW = T + 4 * PAD
N_MEM = 256
MT = len(SEQS) * N_MEM // P
MHEADS, MHD = 4, 256
GROUPS, EPG = 4, 8
NE = GROUPS * EPG
FE = 256
NR = GROUPS + NE
LN_EPS, RMS_EPS = 1e-5, 1e-6
ALPHA = 2.0 ** 0.25
C = P
BLOCKS = T // C
MAX_OVER = (2 * T - 1) // C
PAIRS_OVER = (MAX_OVER + 1) // 2
NB = 4
STEADY = NE + 2
AHEAD = 3
LIST = 2 * PAIRS_OVER
BIG = 4095
SLOT = KC * 512


def weight_slabs(w_in, w_mix, w_ck, w_cv, w_cq, w_co):
    return [("a", w_in[:, 768:1280]), ("g", w_in[:, 1280:1792]), ("q", w_in[:, 0:512]), ("kv", w_in[:, 512:768]),
            ("mix0", w_mix[:, 0:512]), ("mix1", w_mix[:, 512:1024]),
            ("ck0", w_ck[:, 0:512]), ("ck1", w_ck[:, 512:1024]),
            ("cv0", w_cv[:, 0:512]), ("cv1", w_cv[:, 512:1024]),
            ("cq0", w_cq[:, 0:512]), ("cq1", w_cq[:, 512:1024]),
            ("co0", w_co[:, 0:512]), ("co1", w_co[:, 512:1024])]


def self_units():
    out, n = [], 0
    for s, (t0, length) in enumerate(SEQS):
        for pair in range(PAIRS):
            for half in range(KV_HEADS):
                for i in range(length // P):
                    out.append((n, s, pair + PAIRS * half, i, length))
                n += 1
    return out


def cross_units():
    out, n = [], 0
    for s, (t0, length) in enumerate(SEQS):
        for h in range(MHEADS):
            for i in range(length // P):
                out.append((n, s, h, i, N_MEM))
            n += 1
    return out


SELF, CROSS = self_units(), cross_units()
ROT_POOL, ROT_DVE = (2, 3), (0, 1, 4, 5)
CONV_AFTER = {"mean": 4, "var": 5}
QKT_AFTER = {4: (0, 1), 5: (2, 3)}
CUTS = (9, 19)
NTAP = 5
S_AHEAD = 3


def plan_banks():
    place, used, turn = {}, [0] * 8, {}

    def take(kind, key):
        banks = {"mm": (0, 1, 2, 3), "tr": (4, 5), "pv": (6, 7)}[kind]
        b = banks[turn.get(kind, 0) % len(banks)]
        turn[kind] = turn.get(kind, 0) + 1
        place[key] = (b, used[b])
        used[b] += 1

    for i in range(NT):
        for j in range(2):
            take("tr", ("hT", 0, i, j))
    take("tr", "cpar")
    for c in range(CC):
        for s in range(2):
            take("mm", ("a", c, s))
            take("mm", ("g", c, s))
    for i in range(NT):
        take("mm", ("q", i))
        take("mm", ("kv", i))
        for what in ("mean", "var"):
            for s in range(2):
                if i == CONV_AFTER[what]:
                    take("mm", (what, s))
    for i in range(NT):
        take("tr", ("qT", i))
        take("tr", ("kT", i))
    for kind, units in (("s", SELF), ("x", CROSS)):
        if kind == "x":
            for i in range(NT):
                for j in range(2):
                    take("mm", ("mix", i, j))
            for i in range(MT):
                for j in range(2):
                    take("tr", ("hT", 1, i, j))
                for j in range(2):
                    take("tr", ("mT", i, j))
            for c in range(KC):
                take("mm", ("ck", c))
            for i in range(MT):
                for j in range(2):
                    take("mm", ("cv", i, j))
            for i in range(MT, NT):
                for j in range(2):
                    take("tr", ("hT", 1, i, j))
            for c in range(KC):
                for s in range(2):
                    take("mm", ("cq", c, s))
        for u in range(len(units)):
            take("mm", (kind + "S", u))
            take("tr", (kind + "T", u))
        for n in range(units[-1][0] + 1):
            for j in range(1 if kind == "s" else 2):
                take("pv", (kind + "O", n, j))
    for i in range(NT + 1):
        for j in range(2):
            if i < NT:
                take("mm", ("co", i, j))
        for j in range(2):
            if i >= 1:
                take("tr", ("hT", 2, i - 1, j))
    take("pv", "route")
    take("tr", "first")
    for key in ("rank", "count", "base", "list"):
        take("mm", key)
    return place, used


def encoder(nc, x, mem, w_slabs, lnp, rope_cos, rope_sin, q_gain, k_gain, cpar_dram, w_router, b_router,
            w_gate, w_up, w_down, y):
    place, bank_uses = plan_banks()
    slab_names = [n for n, _ in w_slabs]
    h2_dram = nc.dram_tensor("h2_rows", [T, D], F32).ap()
    pair_dram = nc.dram_tensor("pair_rows", [2 * T, D], F32).ap()
    table_dram = nc.dram_tensor("slot_table", [T * NE, 2], I32).ap()

    with ExitStack() as ctx:
        def sb(name, shape, dt=F32):
            return ctx.enter_context(nc.sbuf_tensor(name, shape, dt))

        def sem(name):
            return ctx.enter_context(nc.semaphore(name))

        ps = ctx.enter_context(nc.psum_tensor("ps", [P, 8, 512], F32))

        hres = sb("hres", [P, NT, D])
        hT = sb("hT", [P, KC * T])
        cat = sb("cat", [P, KC * T])
        early = sb("early", [P, 8192])
        scr = sb("scr", [P, 6144])
        ring = sb("ring", [P, 3, SLOT])
        gb = sb("gb", [P, 2, D])
        memx = sb("memx", [P, 2 * D])

        hTv = hT[:, :].rearrange("p (k t) -> p k t", k=KC)
        catv = cat[:, :].rearrange("p (k t) -> p k t", k=KC)
        upad = early[:, 0:CC * UW].rearrange("p (c t) -> p c t", c=CC)
        o = CC * UW
        qT = early[:, o:o + PAIRS * T].rearrange("p (c t) -> p c t", c=PAIRS)
        o += PAIRS * T
        kT = early[:, o:o + T]
        o += T
        vtok = early[:, o:o + NT * P].rearrange("p (i c) -> p i c", i=NT)
        assert o + NT * P <= 8192
        kmT = early[:, 0:4096].rearrange("p (k t) -> p k t", k=KC)
        vm = early[:, 4096:8192].rearrange("p (i c) -> p i c", i=MT)
        sig = scr[:, 0:CC * T].rearrange("p (c t) -> p c t", c=CC)
        raw = [a[:, o:o + 640].rearrange("p (h d) -> p h d", h=NQK) for a, o in
               [(scr, CC * T), (scr, CC * T + 640), (cat, 2304)] + [(ring[:, 0, :], 2048 + 640 * n) for n in range(3)]]
        rtmp = [scr[:, CC * T + 1280 + 320 * n:CC * T + 1280 + 320 * (n + 1)].rearrange("p (h d) -> p h d", h=NQK)
                for n in range(2)]
        cos_raw = scr[:, CC * T + 2560:CC * T + 2688].rearrange("p (i d) -> p i d", i=4)
        sin_raw = scr[:, CC * T + 2688:CC * T + 2816].rearrange("p (i d) -> p i d", i=4)
        tap = [cat[:, 1024 + SEQS[0][1] * n:1024 + SEQS[0][1] * (n + 1)] for n in range(NTAP)]
        rtmp_d = [cat[:, 320 * n:320 * (n + 1)].rearrange("p (h d) -> p h d", h=NQK) for n in range(2)]
        squares = [scr[:, CC * T + 1920:CC * T + 2560], memx[:, 1280:1920]]
        rot = [a[:, o:o + 640] for a, o in ((memx, 0), (memx, 640), (cat, 1024), (cat, 1664))]
        convsq = scr[:, 0:CC * T].rearrange("p (c t) -> p c t", c=CC)
        cstd = scr[:, 0:T]
        PT = [scr[:, 2048 * n:2048 * (n + 1)].rearrange("p (k t) -> p k t", k=4) for n in range(2)]
        prob = [scr[:, 4096 + 512 * n:4096 + 512 * (n + 1)] for n in range(4)]
        mT = scr[:, 0:4096].rearrange("p (k t) -> p k t", k=KC)
        mgb = scr[:, 4096:6144].rearrange("p (a d) -> p a d", a=2)
        mrow = [memx[:, D * n:D * (n + 1)] for n in range(2)]
        acc = catv[:, CC:2 * CC, :]
        ringf = ring[:, :, :].rearrange("p n c -> p (n c)")
        wexp = [early[:, 0:6144], scr[:, 0:6144], ringf[:, 0:6144], cat[:, 0:6144]]
        xg = [hT[:, D * n:D * (n + 1)] for n in range(2)] + [ringf[:, 6144 + D * n:6144 + D * (n + 1)] for n in range(2)]
        xT = [hT[:, D * (2 + n):D * (3 + n)].rearrange("p (k t) -> p k t", k=KC) for n in range(2)]
        yo = [hT[:, D * (4 + n):D * (5 + n)] for n in range(2)]
        hid = [memx[:, 256 * n:256 * (n + 1)].rearrange("p (k t) -> p k t", k=2) for n in range(2)]
        act_g = [memx[:, 512 + 256 * n:512 + 256 * (n + 1)].rearrange("p (k t) -> p k t", k=2) for n in range(2)]
        prow = [(cat if n % 2 == 0 else scr)[:, D * (n // 2):D * (n // 2 + 1)] for n in range(2 * NT)]
        hot = [hT[:, 4096 + NT * P * n:4096 + NT * P * (n + 1)].rearrange("p (t r) -> p t r", t=NT) for n in range(2)]

        ident = sb("ident", [P, P])
        ones = sb("ones", [P, P])
        ones_c = sb("ones_c", [P, P])
        before = sb("before", [P, P])
        qtab = sb("qtab", [P, 4, 4, 32])
        ktab = sb("ktab", [P, 4, 4, 32])
        qkg = sb("qkg", [P, 2, HD])
        cpar_in = sb("cpar_in", [TAPS + 3, CONV])
        cpar = sb("cpar", [P, CC, TAPS + 3])
        epsv = sb("epsv", [P, 2])
        stats = sb("stats", [P, 2, 2, 6])
        mv = sb("mv", [P, 2, 2])
        lnc = sb("lnc", [P, 2, 2])
        lnt = sb("lnt", [P, 1])
        ssq = sb("ssq", [P, NT, NQK])
        rqk = sb("rqk", [P, NT, 2, NQK])
        mhalf = sb("mhalf", [P, NQK])
        nmax = sb("nmax", [P, 4])
        rsum = sb("rsum", [P, 4])
        rinv = sb("rinv", [P, 4])
        wr = sb("wr", [P, KC, NR])
        br = sb("br", [P, NR])[:, :]
        tinit = sb("tinit", [P, T * NE // P * 2], I32)
        tvals = sb("tvals", [P, NT, 2, 2], I32)
        slots = sb("slots", [P, 2, NT], U32)
        tab0 = sb("tab0", [P, 2 * NE], I32)
        tab = sb("tab", [P, BLOCKS * NE * 2 + 2], I32)
        gidx = [sb(f"gidx{n}", [P, 1], U32) for n in range(NB)]
        sidx = [sb(f"sidx{n}", [P, 1], U32) for n in range(2)]
        ctl = sb("ctl", [1, 1 + 2 * LIST], I32)
        pw = sb("pw", [P, 2, NT])

        rt, at = ring[:, 2, :], [0]

        def rv(*shape):
            n = 1
            for k in shape:
                n *= k
            a = rt[:, at[0]:at[0] + n]
            at[0] += n
            if len(shape) == 2:
                return a.rearrange("p (a b) -> p a b", a=shape[0])
            if len(shape) == 3:
                return a.rearrange("p (a b c) -> p a b c", a=shape[0], b=shape[1])
            return a

        lg = rv(NT, NR)
        gmx, gm2, gsum, pgrp = rv(NT), rv(NT), rv(NT), rv(NT)
        geq, G, gex = rv(NT, GROUPS), rv(NT, GROUPS), rv(NT, GROUPS)
        esel4, esel = rv(NT, GROUPS, EPG), rv(NT, EPG)
        v1, v2, m1, m2, ev, den = rv(NT), rv(NT), rv(NT), rv(NT), rv(NT), rv(NT)
        eq, H1, e2, H2 = rv(NT, EPG), rv(NT, EPG), rv(NT, EPG), rv(NT, EPG)
        pick = [rv(NT, GROUPS, EPG), rv(NT, GROUPS, EPG)]
        both = rv(NT, NE)
        upto = rv(NT, NE)
        held = [rv(NT, 2, NE), rv(NT, 2, NE)]
        tokf, pairf = rv(NT), rv(NT)
        riota = rv(P)
        rankf = [rv(NT), rv(NT)]
        rk, rkp = rv(NT, NE), rv(NT, NE)
        slotf = rv(NT)
        desc = rv(EPG)
        eiota = rv(NE)
        cnt, over, base = rv(1), rv(1), rv(1)
        thr = rv(BLOCKS - 1)
        more = rv(BLOCKS - 1)
        jb = rv(BLOCKS - 1, LIST)
        hitm = rv(BLOCKS - 1, LIST)
        bcol = rv(BLOCKS - 1)
        lst = rv(2 * (BLOCKS - 1) * LIST)
        lstb = rv((BLOCKS - 1) * LIST)
        res = rv(1 + 2 * LIST)
        ecol = rv(2)
        assert at[0] <= SLOT

        bank_full = [sem(f"bank_full{b}") for b in range(8)]
        bank_free = [sem(f"bank_free{b}") for b in range(8)]
        first_in = sem("first_in")
        slab_in = [sem(f"slab_in{n}") for n in range(3)]
        x_in = [sem(f"x_in{n}") for n in range(NT)]
        mem_in = [sem(f"mem_in{n}") for n in range(2)]
        gb_in, mgb_in, conv_in, small_in, rope_in = sem("gb_in"), sem("mgb_in"), sem("conv_in"), sem("small_in"), sem("rope_in")
        const_pool, const_ready = sem("const_pool"), sem("const_ready")
        ln_stats, ln_coef, ln_hat, ln_gain, ln_done = (sem(n) for n in
                                                       ("ln_stats", "ln_coef", "ln_hat", "ln_gain", "ln_done"))
        dve_step, pool_step = sem("dve_step"), sem("pool_step")
        conv_done = [sem("conv_done_pool"), sem("conv_done_dve")]
        rqk_ready = sem("rqk_ready")
        u_ready, taps_ready = sem("u_ready"), sem("taps_ready")
        qkv_raw, rot_ready = sem("qkv_raw"), [sem("rot_pool"), sem("rot_dve")]
        tabs_ready = sem("tabs_ready")
        conv_sq, conv_norm, conv_out = sem("conv_sq"), sem("conv_norm"), sem("conv_out")
        max_ready, inv_ready, prob_ready = sem("max_ready"), sem("inv_ready"), sem("prob_ready")
        h2_stored, route_exp, route_const, route_dve = sem("h2_stored"), sem("route_exp"), sem("route_const"), sem("route_dve")
        table_init, slots_ready, table_done, tab_in = sem("table_init"), sem("slots_ready"), sem("table_done"), sem("tab_in")
        counts_in, ctl_ready = sem("counts_in"), sem("ctl_ready")
        wexp_in = [sem(f"wexp_in{n}") for n in range(NB)]
        rows_in = [sem(f"rows_in{n}") for n in range(NB)]
        rows_out = [sem(f"rows_out{n}") for n in range(2)]
        gidx_ready, sidx_ready, index_seen = sem("gidx_ready"), sem("sidx_ready"), sem("index_seen")
        rowsT_full, rowsT_a, rowsT_d = sem("rowsT_full"), sem("rowsT_a"), sem("rowsT_d")
        gu_full, silu_done, hid_ready, down_full, yo_a, yo_d = (
            sem(n) for n in ("gu_full", "silu_done", "hid_ready", "down_full", "yo_a", "yo_d"))
        hot_ready, tab0_ready = sem("hot_ready"), sem("tab0_ready")
        prow_in = [sem(f"prow_in{n}") for n in range(2 * NT)]
        summed = sem("summed")
        prow_used, y_out, scaled = sem("prow_used"), sem("y_out"), sem("scaled")

        block = ctx.enter_context(nc.Block())

        def full(eng, key):
            b, n = place[key]
            eng.wait_ge(bank_full[b], n + 1)
            return ps[:, b, :]

        def was_read(eng, key):
            b, n = place[key]
            eng.wait_ge(bank_free[b], n + 1)

        def later(n):
            return not isinstance(n, int) or n >= 1

        def free(key):
            return bank_free[place[key][0]]

        slab_last = {"a": ("a", CC - 1, 1), "g": ("g", CC - 1, 1), "q": ("q", NT - 1), "kv": ("kv", NT - 1)}
        for j in range(2):
            slab_last |= {f"mix{j}": ("mix", NT - 1, j), f"ck{j}": ("ck", 4 * j + 3), f"cv{j}": ("cv", MT - 1, j),
                          f"cq{j}": ("cq", 4 * j + 3, 1), f"co{j}": ("co", NT - 1, j)}

        LN_X = list(range(NT))
        LN_1 = [NT + n for n in (0, 2, 4, 6, 8, 9)]
        LN_M = [NT + n for n in (1, 3, 5, 7)]
        LN_2 = [LN_1[-1] + 1 + i for i in range(NT)]
        LN_3 = [LN_2[-1] + 1 + i for i in range(NT)]
        SHORT = (LN_X[0], LN_X[1], LN_2[-1], LN_3[-1])

        def shared(n):
            return n + 1 - len([m for m in SHORT if m <= n])

        @block.sync
        def _(sp):
            def bcast(v):
                return v.rearrange("(a d) -> a d", a=1).to_broadcast([P, v.shape[0]])

            def load_gb(n):
                sp.dma_start(gb[:, 0, :], bcast(lnp[2 * n])).then_inc(gb_in, 16)
                sp.dma_start(gb[:, 1, :], bcast(lnp[2 * n + 1])).then_inc(gb_in, 16)

            def chunks(w, in_dram=False):
                return w.rearrange("(k p) c -> p k c", p=P) if in_dram else w.rearrange("p (k c) -> p k c", k=KC)

            def load_slab(n):
                w = w_slabs[n][1]
                if n >= 3:
                    full(sp, slab_last[slab_names[n - 3]])
                dst = ring[:, n % 3, 0:KC * w.shape[1]].rearrange("p (k c) -> p k c", k=KC)
                sp.dma_start(dst, w.rearrange("(k p) c -> p k c", p=P)).then_inc(slab_in[n % 3], 16)

            sp.dma_start(hres[:, 0, :], x[0:P, :]).then_inc(x_in[0], 16)
            load_gb(0)
            for i in range(1, NT):
                sp.dma_start(hres[:, i, :], x[i * P:(i + 1) * P, :]).then_inc(x_in[i], 16)
                if i == 1:
                    for n in range(2):
                        sp.dma_start(chunks(ring[:, n, :])[:, :, 0:P],
                                     chunks(w_slabs[n][1], True)[:, :, 0:P]).then_inc(first_in, 16)
            for n in range(2):
                sp.dma_start(chunks(ring[:, n, :])[:, :, P:512],
                             chunks(w_slabs[n][1], True)[:, :, P:512]).then_inc(slab_in[n], 16)
            sp.dma_start(cpar_in[:, :], cpar_dram).then_inc(conv_in, 16)
            sp.dma_start(qkg[:, 0, :], bcast(q_gain)).then_inc(rope_in, 16)
            sp.dma_start(qkg[:, 1, :], bcast(k_gain)).then_inc(rope_in, 16)
            sp.dma_start(cos_raw, rope_cos.rearrange("(i p) d -> p i d", p=P)).then_inc(rope_in, 16)
            sp.dma_start(sin_raw, rope_sin.rearrange("(i p) d -> p i d", p=P)).then_inc(rope_in, 16)
            load_slab(2)
            sp.dma_start(wr[:, :, :], w_router).then_inc(small_in, 16)
            sp.dma_start(br, bcast(b_router)).then_inc(small_in, 16)
            sp.wait_ge(const_ready, 2)
            sp.dma_start(table_dram.rearrange("(p n) t -> p (n t)", p=P), tinit[:, :]).then_inc(table_init, 16)
            sp.wait_ge(ln_done, NT)
            load_gb(1)
            for n in range(3, 6):
                load_slab(n)
            full(sp, ("kT", NT - 1))
            for i in range(2):
                sp.dma_start(mrow[i], mem[i * P:(i + 1) * P, :]).then_inc(mem_in[i], 16)
            full(sp, ("sO", SELF[-1][0], 0))
            for j in range(2):
                sp.dma_start(mgb[:, j, :], bcast(lnp[2 + 6 + j])).then_inc(mgb_in, 16)
            load_slab(6)
            for i in range(2, MT):
                full(sp, ("mT", i - 2, 1))
                sp.dma_start(mrow[i % 2], mem[i * P:(i + 1) * P, :]).then_inc(mem_in[i % 2], 16)
            for n in range(7, 9):
                load_slab(n)
            sp.wait_ge(ln_done, LN_1[-1] + 1)
            load_gb(2)
            for n in range(9, len(w_slabs)):
                load_slab(n)
            full(sp, ("xO", CROSS[-1][0], 1))

            def load_expert(b, e):
                for off, w in ((0, w_gate), (2048, w_up)):
                    sp.dma_start(wexp[b][:, off:off + 2048],
                                 w[bass.ds(e, 1)].rearrange("e (p k) f -> p (e k f)", p=P)).then_inc(wexp_in[b], 16)
                sp.dma_start(wexp[b][:, 4096:6144],
                             w_down[bass.ds(e, 1)].rearrange("e (p k) f -> p (e k f)", p=P)).then_inc(wexp_in[b], 16)

            for e in range(2):
                load_expert(e, e)
            for i in range(NT):
                sp.wait_ge(ln_done, LN_2[i] + 1)
                sp.dma_start(h2_dram[i * P:(i + 1) * P, :], hres[:, i, :]).then_inc(h2_stored, 16)
            full(sp, ("co", NT - 1, 1))
            load_expert(2, 2)
            load_gb(3)
            full(sp, "route")
            load_expert(3, 3)
            with sp.Fori(1, NE // NB) as i:
                for b in range(NB):
                    sp.wait_ge(down_full, NB * i + b - NB + 1)
                    load_expert(b, NB * i + b)
            sp.wait_ge(table_done, 16 * 2 * NT)
            sp.dma_start(tab[:, 0:BLOCKS * NE * 2].rearrange("p (b c) -> p b c", b=BLOCKS),
                         table_dram.rearrange("(b p e) t -> p b (e t)", p=P, b=BLOCKS)).then_inc(tab_in, 16)
            sp.wait_ge(ctl_ready, 1)
            for b in range(2):
                e = sp.value_load(ctl[0:1, 1 + b:2 + b], min_val=0, max_val=NE - 1)
                sp.wait_ge(down_full, NE - NB + b + 1)
                load_expert(b, e)
            n_over = sp.value_load(ctl[0:1, 0:1], min_val=0, max_val=LIST)
            with sp.Fori(1, PAIRS_OVER) as i:
                with sp.If(2 * i < n_over):
                    for b in range(2):
                        e = sp.value_load(ctl[0:1, bass.ds(1 + 2 * i + b, 1)], min_val=0, max_val=NE - 1)
                        sp.wait_ge(down_full, NE + 2 * i + b - 1)
                        load_expert(b, e)
            sp.wait_ge(prow_used, 1)
            for i in range(NT):
                for k in range(2):
                    n, r = 2 * i + k, k * T + i * P
                    sp.dma_start(prow[n], pair_dram[r:r + P, :]).then_inc(prow_in[n], 16)
            for i in range(NT):
                sp.wait_ge(ln_done, LN_3[i] + 1)
                sp.dma_start(y[i * P:(i + 1) * P, :], hres[:, i, :]).then_inc(y_out, 16)
            sp.wait_ge(y_out, 16 * NT)

        def ln_rows(n):
            if n in LN_M:
                return mrow[LN_M.index(n) % 2], mgb[:, 0, :], mgb[:, 1, :]
            for ns in (LN_X, LN_1, LN_2, LN_3):
                if n in ns:
                    return hres[:, ns.index(n), :], gb[:, 0, :], gb[:, 1, :]

        def gb_wait(eng, n):
            if n in LN_M:
                eng.wait_ge(mgb_in, 32)
            else:
                eng.wait_ge(gb_in, 32 * (1 + [n in ns for ns in (LN_X, LN_1, LN_2, LN_3)].index(True)))

        def pool_coef(pool, n, link):
            pool.wait_ge(ln_stats, n + 1)
            if n - 2 in SHORT:
                pool.wait_ge(ln_done, n - 1)
            elif n >= 2:
                pool.wait_ge(ln_hat, shared(n - 2))
            link(nc.gpsimd.tensor_scalar(lnt[:, :], mv[:, n % 2, 1:2], LN_EPS, None, ALU.add))
            link(nc.gpsimd.tensor_tensor(lnc[:, n % 2, 0:1], lnt[:, :], mhalf[:, 0:1], ALU.pow))
            nc.gpsimd.tensor_scalar(lnc[:, n % 2, 1:2], mv[:, n % 2, 0:1], lnc[:, n % 2, 0:1], -1.0,
                                    ALU.mult, ALU.mult).then_inc(ln_coef, 1)

        def pool_gain(pool, n):
            if n in SHORT:
                return
            rows, g, _ = ln_rows(n)
            gb_wait(pool, n)
            pool.wait_ge(ln_hat, shared(n))
            nc.gpsimd.tensor_tensor(rows, rows, g, ALU.mult).then_inc(ln_gain, 1)

        def act_hat(act, n):
            if n in SHORT:
                return
            rows, _, _ = ln_rows(n)
            act.wait_ge(ln_coef, n + 1)
            nc.scalar.activation(rows, rows, ACT.Identity, bias=lnc[:, n % 2, 1:2],
                                 scale=lnc[:, n % 2, 0:1]).then_inc(ln_hat, 1)

        def dve_stats(dve, n, link):
            rows, _, _ = ln_rows(n)
            if n >= 2:
                dve.wait_ge(ln_coef, n - 1)
            for j in range(2):
                last = nc.vector.bn_stats(stats[:, n % 2, j, :], rows[:, 512 * j:512 * (j + 1)])
            link(last)
            nc.vector.bn_aggr(mv[:, n % 2, :], stats[:, n % 2, :, :]).then_inc(ln_stats, 1)
            if n in SHORT:
                dve.wait_ge(ln_stats, n + 1)

        def dve_bias(dve, n, link):
            rows, g, b = ln_rows(n)
            gb_wait(dve, n)
            if n in SHORT:
                link(nc.vector.scalar_tensor_tensor(out=rows, in0=rows, scalar=mv[:, n % 2, 0:1], in1=g,
                                                    op0=ALU.subtract, op1=ALU.mult))
                dve.wait_ge(ln_coef, n + 1)
                nc.vector.scalar_tensor_tensor(out=rows, in0=rows, scalar=lnc[:, n % 2, 0:1], in1=b,
                                               op0=ALU.mult, op1=ALU.add).then_inc(ln_done, 1)
                return
            dve.wait_ge(ln_gain, shared(n))
            nc.vector.tensor_tensor(rows, rows, b, ALU.add).then_inc(ln_done, 1)

        def rotate(eng, e, i, tmp, link):
            pos = i - SEQS[TILES[i][0]][0] // P
            r, rs2 = raw[i], rqk[:, i, :, :]
            eng.wait_ge(rqk_ready, i + 1)
            rs = rs2[:, 1, :].rearrange("p (h a) -> p h a", a=1).to_broadcast([P, NQK, HD])
            link(e.tensor_tensor(r, r, rs, ALU.mult))
            if i >= 4:
                full(eng, ("kT", i - 4))
            out = rot[i % 4]
            qo = out[:, 0:HEADS * HD].rearrange("p (c a d) -> p a c d", c=PAIRS, a=2)
            ko = out[:, HEADS * HD:NQK * HD].rearrange("p (a c d) -> p a c d", a=2, c=1)
            for odd in range(2):
                for n, tabx, h0, h1 in ((0, qtab, 0, HEADS), (1, ktab, HEADS, NQK)):
                    for m in range(2):
                        t = tabx[:, pos, 2 * odd + m:2 * odd + m + 1, :].to_broadcast([P, h1 - h0, 32])
                        last = e.tensor_tensor(tmp[m][:, h0:h1, :], r[:, h0:h1, m:HD:2], t, ALU.mult)
                link(last)
                for a in range(2):
                    last = e.tensor_tensor(qo[:, a, :, odd:HD:2], tmp[0][:, 4 * a:4 * a + 4, :],
                                           tmp[1][:, 4 * a:4 * a + 4, :], ALU.add if odd else ALU.subtract)
                last = e.tensor_tensor(ko[:, :, 0, odd:HD:2], tmp[0][:, HEADS:NQK, :], tmp[1][:, HEADS:NQK, :],
                                       ALU.add if odd else ALU.subtract)
                if odd == 0:
                    link(last)
            last.then_inc(rot_ready[i in ROT_DVE], 1)

        def rotated(eng, i):
            by = (ROT_POOL, ROT_DVE)[i in ROT_DVE]
            eng.wait_ge(rot_ready[i in ROT_DVE], by.index(i) + 1)

        @block.gpsimd
        def _(pool):
            steps = [0]

            def link(ins):
                steps[0] += 1
                ins.then_inc(pool_step, 1)
                pool.wait_ge(pool_step, steps[0])

            g = nc.gpsimd
            link(g.memset(mhalf[:, :], -0.5))
            g.memset(ones[:, :], 1.0).then_inc(const_pool, 1)
            g.memset(ident[:, :], 0.0).then_inc(const_pool, 1)
            g.memset(ones_c[:, :], 1.0 / CONV).then_inc(const_pool, 1)
            g.memset(epsv[:, :], LN_EPS).then_inc(const_pool, 1)
            pool.wait_ge(const_pool, 4)
            g.affine_select(out=ident[:, :], in_=ident[:, :], compare_op=ALU.not_equal, fill=1.0, base=0,
                            pattern=[[-1, P]], channel_multiplier=1).then_inc(const_pool, 1)
            g.affine_select(out=before[:, :], in_=ones[:, :], compare_op=ALU.is_gt, fill=0.0, base=0,
                            pattern=[[1, P]], channel_multiplier=-1).then_inc(const_pool, 1)
            pool.wait_ge(const_pool, 6)
            g.memset(upad, 0.0).then_inc(const_ready, 1)
            g.iota(tvals[:, :, :, 0], pattern=[[P, NT], [0, 2]], base=0, channel_multiplier=1).then_inc(const_pool, 1)
            g.iota(tvals[:, :, :, 1], pattern=[[P, NT], [T, 2]], base=0, channel_multiplier=1).then_inc(const_pool, 1)
            pool.wait_ge(const_pool, 8)
            link(g.iota(tab[:, BLOCKS * NE * 2:], pattern=[[0, 2]], base=BIG, channel_multiplier=0))
            g.iota(tinit[:, :], pattern=[[0, T * NE // P * 2]], base=BIG, channel_multiplier=0).then_inc(const_ready, 1)

            def norms(ns, lag=1):
                for k, n in enumerate(ns):
                    pool_coef(pool, n, link)
                    if k >= lag:
                        pool_gain(pool, ns[k - lag])
                for n in ns[len(ns) - lag:]:
                    pool_gain(pool, n)

            norms(LN_X)

            pool.wait_ge(rope_in, 64)
            for tabx, gi in ((qtab, 0), (ktab, 1)):
                for m, (src, odd) in enumerate(((cos_raw, 0), (sin_raw, 1), (sin_raw, 0), (cos_raw, 1))):
                    gain = qkg[:, gi:gi + 1, odd:HD:2].to_broadcast([P, 4, 32])
                    link(g.tensor_tensor(tabx[:, :, m, :], src, gain, ALU.mult))
            pool.sem_inc(tabs_ready, 1)

            def factors(i):
                rs2 = rqk[:, i, :, :]
                pool.wait_ge(qkv_raw, i + 1)
                link(g.tensor_scalar(rs2[:, 0, :], ssq[:, i, :], 1.0 / HD, RMS_EPS, ALU.mult, ALU.add))
                link(g.tensor_tensor(rs2[:, 1, :], rs2[:, 0, :], mhalf[:, :], ALU.pow))
                g.tensor_scalar(rs2[:, 1, 0:HEADS], rs2[:, 1, 0:HEADS], HD ** -0.5, None,
                                ALU.mult).then_inc(rqk_ready, 1)

            length = SEQS[0][1]
            for c in range(CC):
                was_read(pool, ("a", c, 0))
                was_read(pool, ("g", c, 0))
                gated = upad[:, c, PAD:PAD + length]
                g.tensor_tensor(gated, gated, sig[:, c, 0:length], ALU.mult).then_inc(u_ready, 1)
                for k in range(1, TAPS):
                    n = c * (TAPS - 1) + k - 1
                    pool.wait_ge(taps_ready, c * TAPS + k + 1)
                    if k > 1:
                        pool.wait_ge(conv_done[0], n)
                    g.tensor_tensor(acc[:, c, 0:length], acc[:, c, 0:length], tap[n % NTAP],
                                    ALU.add).then_inc(conv_done[0], 1)
                    if c == CC - 1 and k == TAPS - 6:
                        factors(0)
                        factors(1)
            for i in range(2, NT):
                factors(i)
                if i == 2 or i == 4:
                    rotate(pool, g, ROT_POOL[i // 2 - 1], rtmp, link)

            def normalise(units, u0):
                for u in range(len(units)):
                    width = units[u][4]
                    pool.wait_ge(inv_ready, u0 + u + 1)
                    g.tensor_scalar(prob[u % 4][:, 0:width], prob[u % 4][:, 0:width], rinv[:, u % 4:u % 4 + 1],
                                    None, ALU.mult).then_inc(prob_ready, 1)

            normalise(SELF, 0)
            norms(sorted(LN_1 + LN_M))
            normalise(CROSS, len(SELF))

            for a, st in ((desc, (-1, EPG, EPG)), (eiota, (1, NE, 0)), (thr, (C, BLOCKS - 1, C)),
                          (bcol, (NE, BLOCKS - 1, NE - BLOCKS * NE)), (riota, (1, P, 0))):
                g.iota(a, pattern=[[st[0], st[1]]], base=st[2], channel_multiplier=0,
                       allow_small_or_imprecise_dtypes=True).then_inc(route_const, 1)
            g.iota(jb, pattern=[[-1, BLOCKS - 1], [1, LIST]], base=0, channel_multiplier=0,
                   allow_small_or_imprecise_dtypes=True).then_inc(route_const, 1)
            g.iota(ecol[:, 0:1], pattern=[[0, 1]], base=0, channel_multiplier=1,
                   allow_small_or_imprecise_dtypes=True).then_inc(route_const, 1)
            for a, row0 in ((tokf, 0), (pairf, T)):
                g.iota(a, pattern=[[P, NT]], base=row0 - BIG, channel_multiplier=1,
                       allow_small_or_imprecise_dtypes=True).then_inc(route_const, 1)

            norms(LN_2, lag=0)

            last_token, last_pair = pool.to_reg(T - 1), pool.to_reg(2 * T - 1)

            def gather(j, b, col):
                if later(j - b):
                    pool.wait_ge(rowsT_full, j - NB + 1)
                g.tensor_copy(gidx[b][:, :], col[0]).then_inc(gidx_ready, 1)
                pool.wait_ge(gidx_ready, j + 1)
                pool.sem_inc(index_seen, 1)
                g.indirect_dma_start(xg[b], None, h2_dram, bass.IndirectOffsetOnAxis(ap=gidx[b][:, :], axis=0),
                                     bounds_check=last_token, oob_is_err=False).then_inc(rows_in[b], 16)

            def scatter(j, b, col, uses):
                if later(uses):
                    pool.wait_ge(rows_out[b], 16 * uses)
                g.tensor_copy(sidx[b][:, :], col[1]).then_inc(sidx_ready, 1)
                pool.wait_ge(sidx_ready, j + 1)
                pool.wait_ge(yo_a, j + 1)
                pool.wait_ge(yo_d, j + 1)
                pool.sem_inc(index_seen, 1)
                g.indirect_dma_start(pair_dram, bass.IndirectOffsetOnAxis(ap=sidx[b][:, :], axis=0), yo[b], None,
                                     bounds_check=last_pair, oob_is_err=False).then_inc(rows_out[b], 16)

            def col(c):
                return tab[:, bass.ds(2 * c, 1)], tab[:, bass.ds(2 * c + 1, 1)]

            def first(e):
                return tab0[:, bass.ds(e, 1)], tab0[:, bass.ds(NE + e, 1)]

            pool.wait_ge(h2_stored, 16 * NT)
            pool.wait_ge(tab0_ready, 1)
            full(pool, ("co", NT - 1, 1))

            def quad(i):
                for b in range(NB):
                    j = NB * i + b
                    gather(j + AHEAD, (b + AHEAD) % NB, first(j + AHEAD))
                    scatter(j, b % 2, first(j), 2 * i + b // 2)

            for j in range(AHEAD):
                gather(j, j, first(j))
            pool.wait_ge(table_init, 16)
            for k in range(2):
                pool.wait_ge(slots_ready, k + 1)
                for i in range(NT):
                    g.indirect_dma_start(table_dram, bass.IndirectOffsetOnAxis(ap=slots[:, k, i:i + 1], axis=0),
                                         tvals[:, i, k, :], None, bounds_check=T * NE - 1,
                                         oob_is_err=False).then_inc(table_done, 16)
            quad(0)
            with pool.Fori(1, NE // NB - 1) as i:
                quad(i)
            pool.wait_ge(ctl_ready, 1)
            listed = [pool.value_load(ctl[0:1, 1 + LIST + b:2 + LIST + b], min_val=0, max_val=BLOCKS * NE)
                      for b in range(STEADY - NE)]
            cols = {j: first(j) if j < NE else col(listed[j - NE]) for j in range(NE - NB, STEADY)}
            pool.wait_ge(tab_in, 16)
            for j in range(NE - NB, STEADY):
                if j + AHEAD < STEADY:
                    gather(j + AHEAD, (j + AHEAD) % NB, cols[j + AHEAD])
                scatter(j, j % 2, cols[j], j // 2)
            for b in range(2):
                pool.wait_ge(rows_out[b], 16 * (STEADY // 2))
            n_over = pool.value_load(ctl[0:1, 0:1], min_val=0, max_val=LIST)
            with pool.If(n_over > STEADY - NE):
                with pool.Fori(1, PAIRS_OVER) as i:
                    with pool.If(2 * i < n_over):
                        cs = [pool.value_load(ctl[0:1, bass.ds(1 + LIST + 2 * i + b, 1)], min_val=0,
                                              max_val=BLOCKS * NE) for b in range(2)]
                        for b in range(2):
                            gather(NE + 2 * i + b, b, col(cs[b]))
                        for b in range(2):
                            scatter(NE + 2 * i + b, b, col(cs[b]), NE // 2 + i)
                        for b in range(2):
                            pool.wait_ge(rows_out[b], 16 * (NE // 2 + 1 + i))
            pool.sem_inc(prow_used, 1)

            norms(LN_3)

        @block.scalar
        def _(act):
            a = nc.scalar

            def transposed_out(key, dst, n=4):
                bank = full(act, key)
                a.activation(dst, bank[:, 0:n * P].rearrange("p (k t) -> p k t", k=n), ACT.Copy)

            act.wait_ge(const_ready, 1)
            def rows_T(layer, i):
                for j in range(2):
                    key = ("hT", layer, i, j)
                    bank = full(act, key)
                    dst = (catv if layer == 2 else hTv)[:, 4 * j:4 * j + 4, i * P:(i + 1) * P]
                    a.activation(dst, bank.rearrange("p (k t) -> p k t", k=4), ACT.Copy).then_inc(free(key), 1)

            def gate(c, s):
                t0, length = SEQS[s]
                u0 = t0 + PAD + 2 * PAD * s
                bank = full(act, ("a", c, s))
                a.activation(upad[:, c, u0:u0 + length], bank[:, 0:length], ACT.Copy).then_inc(free(("a", c, s)), 1)
                bank = full(act, ("g", c, s))
                a.activation(sig[:, c, t0:t0 + length], bank[:, 0:length], ACT.Sigmoid).then_inc(free(("g", c, s)), 1)

            rows_T(0, 0)
            rows_T(0, 1)
            for n in LN_X[2:]:
                act_hat(act, n)
            gate(0, 0)
            for i in range(2, NT):
                rows_T(0, i)
            bank = full(act, "cpar")
            a.activation(cpar[:, :, :], bank[:, 0:CC * (TAPS + 3)].rearrange("p (c n) -> p c n", c=CC),
                         ACT.Copy).then_inc(free("cpar"), 1)

            def taps(c, k0, k1):
                length = SEQS[0][1]
                act.wait_ge(u_ready, c + 1)
                for k in range(k0, k1):
                    n = c * (TAPS - 1) + k - 1
                    src = upad[:, c, k:k + length]
                    if k == 0:
                        a.activation(acc[:, c, 0:length], src, ACT.Identity, bias=cpar[:, c, TAPS:TAPS + 1],
                                     scale=cpar[:, c, 0:1]).then_inc(taps_ready, 1)
                        continue
                    if n >= NTAP:
                        act.wait_ge(conv_done[0], n - NTAP + 1)
                    a.activation(tap[n % NTAP], src, ACT.Copy, scale=cpar[:, c, k:k + 1]).then_inc(taps_ready, 1)

            was_read(act, "cpar")
            taps(0, 0, CUTS[0])
            gate(0, 1)
            for c in range(CC - 1):
                cuts = CUTS if c else (TAPS // 2, TAPS)
                taps(c, 0 if c else CUTS[0], cuts[0])
                gate(c + 1, 0)
                taps(c, cuts[0], cuts[1])
                gate(c + 1, 1)
                taps(c, cuts[1], TAPS)

            def qk_T(i):
                for key, dst, n in ((("qT", i), qT[:, :, i * P:(i + 1) * P], 4), (("kT", i), kT[:, i * P:(i + 1) * P], 1)):
                    bank = full(act, key)
                    src = bank.rearrange("p (k t) -> p k t", k=4) if n == 4 else bank[:, 0:P]
                    a.activation(dst, src, ACT.Copy).then_inc(free(key), 1)

            for i in range(NT):
                r = raw[i]
                bank = full(act, ("q", i))
                for h in range(HEADS):
                    a.activation(squares[i % 2][:, h * HD:(h + 1) * HD], bank[:, h * HD:(h + 1) * HD], ACT.Square,
                                 accum_out=ssq[:, i, h:h + 1])
                a.activation(r[:, 0:HEADS, :], bank.rearrange("p (h d) -> p h d", h=HEADS),
                             ACT.Copy).then_inc(free(("q", i)), 1)
                bank = full(act, ("kv", i))
                for h in range(KV_HEADS):
                    a.activation(squares[i % 2][:, (HEADS + h) * HD:(HEADS + h + 1) * HD],
                                 bank[:, h * HD:(h + 1) * HD], ACT.Square,
                                 accum_out=ssq[:, i, HEADS + h:HEADS + h + 1])
                a.activation(r[:, HEADS:NQK, :], bank[:, 0:P].rearrange("p (h d) -> p h d", h=KV_HEADS),
                             ACT.Copy).then_inc(qkv_raw, 1)
                a.activation(vtok[:, i, :], bank[:, P:2 * P], ACT.Copy).then_inc(free(("kv", i)), 1)
                if i < 2:
                    taps(CC - 1, (0, CUTS[0])[i], (CUTS[0], TAPS)[i])
                for m in QKT_AFTER.get(i, ()):
                    qk_T(m)
                if i == CONV_AFTER["mean"]:
                    for s, (t0, length) in enumerate(SEQS):
                        was_read(act, ("mean", s))
                        a.activation(convsq[:, :, t0:t0 + length], acc[:, :, t0:t0 + length],
                                     ACT.Square).then_inc(conv_sq, 1)
                if i == CONV_AFTER["var"]:
                    for s, (t0, length) in enumerate(SEQS):
                        bank = full(act, ("var", s))
                        a.activation(cstd[:, t0:t0 + length], bank[:, 0:length], ACT.Sqrt,
                                     bias=epsv[:, 0:1]).then_inc(free(("var", s)), 1)
            for c in range(CC):
                act.wait_ge(conv_norm, c + 1)
                a.activation(acc[:, c, :], acc[:, c, :], ACT.Silu, bias=cpar[:, c, TAPS + 2:TAPS + 3],
                             scale=cpar[:, c, TAPS + 1:TAPS + 2]).then_inc(conv_out, 1)
            for m in (NT - 2, NT - 1):
                qk_T(m)

            def exps(kind, units, u0):
                done = []

                def head_out(n):
                    s, h = next((s, h) for m, s, h, _, _ in units if m == n)
                    t0, length = SEQS[s]
                    if kind == "s":
                        key, half = ("sO", n, 0), h % 2 * HD
                        full(act, key)
                        b = place[key][0]
                        a.activation(catv[half:half + HD, h // 2, t0:t0 + length],
                                     ps[half:half + HD, b, 0:length], ACT.Copy).then_inc(free(key), 1)
                    else:
                        for j in range(2):
                            key = ("xO", n, j)
                            bank = full(act, key)
                            a.activation(hTv[:, 2 * h + j, t0:t0 + length], bank[:, 0:length],
                                         ACT.Copy).then_inc(free(key), 1)

                for u, (n, s, h, i, width) in enumerate(units):
                    last = u - S_AHEAD - 2
                    if last >= 0 and units[last][0] != units[last + 1][0]:
                        head_out(units[last][0])
                        done.append(units[last][0])
                    act.wait_ge(max_ready, u0 + u + 1)
                    if u >= 4:
                        full(act, (kind + "T", u - 4))
                    key = (kind + "S", u)
                    a.activation(prob[u % 4][:, 0:width], ps[:, place[key][0], 0:width], ACT.Exp,
                                 bias=nmax[:, u % 4:u % 4 + 1],
                                 accum_out=rsum[:, u % 4:u % 4 + 1]).then_inc(free(key), 1)
                for n in range(units[-1][0] + 1):
                    if n not in done:
                        head_out(n)

            exps("s", SELF, 0)

            def mem_T(i):
                for j in range(2):
                    key = ("mT", i, j)
                    bank = full(act, key)
                    a.activation(mT[:, 4 * j:4 * j + 4, i * P:(i + 1) * P], bank.rearrange("p (k t) -> p k t", k=4),
                                 ACT.Copy).then_inc(free(key), 1)

            for i in range(NT):
                if i >= 2:
                    rows_T(1, i - 2)
                    mem_T(i - 2)
                act_hat(act, LN_1[i])
                if i < MT:
                    act_hat(act, LN_M[i])
            for c in range(KC):
                bank = full(act, ("ck", c))
                a.activation(kmT[:, c, :], bank, ACT.Copy).then_inc(free(("ck", c)), 1)
            for i in range(MT):
                for j in range(2):
                    bank = full(act, ("cv", i, j))
                    a.activation(vm[:, i, 512 * j:512 * (j + 1)], bank, ACT.Copy).then_inc(free(("cv", i, j)), 1)
            for i in range(MT, NT):
                rows_T(1, i)
            for c in range(KC):
                for s, (t0, length) in enumerate(SEQS):
                    bank = full(act, ("cq", c, s))
                    a.activation(catv[:, c, t0:t0 + length], bank[:, 0:length], ACT.Copy,
                                 scale=MHD ** -0.5).then_inc(free(("cq", c, s)), 1)
            exps("x", CROSS, len(SELF))
            for k, n in enumerate(LN_2):
                if k >= 1:
                    rows_T(2, k - 1)
                act_hat(act, n)
            rows_T(2, NT - 1)

            act.wait_ge(h2_stored, 16 * NT)
            for i in range(NT):
                was_read(act, ("hT", 2, i, 1))
                a.activation(hres[:, i, :], hres[:, i, :], ACT.Copy, scale=ALPHA).then_inc(scaled, 1)
            act.wait_ge(route_dve, 1)
            a.activation(gex, gex, ACT.Exp).then_inc(route_exp, 1)
            act.wait_ge(route_dve, 2)
            a.activation(ev, ev, ACT.Exp).then_inc(route_exp, 1)

            def block_act_T(j, b):
                act.wait_ge(rowsT_full, j + 1)
                a.activation(xT[b][:, 0:4, :], ps[:, 4, :].rearrange("p (k t) -> p k t", k=4),
                             ACT.Copy).then_inc(rowsT_a, 1)

            def block_act(j, b, uses):
                act.wait_ge(gu_full, j + 1)
                if later(uses):
                    act.wait_ge(hid_ready, j - 1)
                a.activation(act_g[b], ps[:, b, 0:256].rearrange("p (k t) -> p k t", k=2),
                             ACT.Silu).then_inc(silu_done, 1)

            def block_act_out(j, b, uses):
                act.wait_ge(down_full, j + 1)
                if later(uses):
                    act.wait_ge(rows_out[b], 16 * uses)
                a.activation(yo[b][:, 0:512], ps[:, 2 + 4 * b, :], ACT.Copy).then_inc(yo_a, 1)

            def blocks(j0, n, half, end=False):
                for b in range(n):
                    block_act(j0 + b, b % 2, half + b // 2)
                    if not (end and b == n - 1):
                        block_act_T(j0 + b + 1, (b + 1) % 2)
                    block_act_out(j0 + b, b % 2, half + b // 2)

            block_act_T(0, 0)
            blocks(0, NB, 0)
            with act.Fori(1, NE // NB - 1) as i:
                blocks(NB * i, NB, 2 * i)
            blocks(NE - NB, NB + STEADY - NE, (NE - NB) // 2, end=True)
            act.wait_ge(ctl_ready, 1)
            n_over = act.value_load(ctl[0:1, 0:1], min_val=0, max_val=LIST)
            with act.Fori(1, PAIRS_OVER) as i:
                with act.If(2 * i < n_over):
                    for b in range(2):
                        block_act_T(NE + 2 * i + b, b)
                        block_act(NE + 2 * i + b, b, NE // 2 + i)
                        block_act_out(NE + 2 * i + b, b, NE // 2 + i)
            for n in LN_3:
                act_hat(act, n)

        @block.vector
        def _(dve):
            v = nc.vector
            steps = [0]

            def link(ins):
                steps[0] += 1
                ins.then_inc(dve_step, 1)
                dve.wait_ge(dve_step, steps[0])

            for n in LN_X:
                dve.wait_ge(x_in[n], 16)
                dve_stats(dve, n, link)
                if n in SHORT:
                    dve_bias(dve, n, link)
                elif n - 2 not in SHORT:
                    dve_bias(dve, n - 2, link)
            for n in LN_X[-2:]:
                dve_bias(dve, n, link)

            t0, length = SEQS[1]
            u0 = t0 + 2 * PAD
            for c in range(CC):
                was_read(dve, ("a", c, 1))
                was_read(dve, ("g", c, 1))
                gated = upad[:, c, u0 + PAD:u0 + PAD + length]
                link(v.tensor_tensor(gated, gated, sig[:, c, t0:t0 + length], ALU.mult))
                if c == 0:
                    was_read(dve, "cpar")
                dst = acc[:, c, t0:t0 + length]
                for k in range(TAPS):
                    src = upad[:, c, u0 + k:u0 + k + length]
                    if k == 0:
                        ins = v.tensor_scalar(dst, src, cpar[:, c, 0:1], cpar[:, c, TAPS:TAPS + 1], ALU.mult, ALU.add)
                    else:
                        dve.wait_ge(conv_done[1], c * TAPS + k)
                        ins = v.scalar_tensor_tensor(out=dst, in0=src, scalar=cpar[:, c, k:k + 1], in1=dst,
                                                     op0=ALU.mult, op1=ALU.add)
                    ins.then_inc(conv_done[1], 1)
            dve.wait_ge(tabs_ready, 1)
            for i in ROT_DVE[0:2]:
                rotate(dve, v, i, rtmp_d, link)
            dve.wait_ge(conv_done[0], CC * (TAPS - 1))
            dve.wait_ge(conv_done[1], CC * TAPS)
            mean = [full(dve, ("mean", s)) for s in range(2)]
            for s, (t0, length) in enumerate(SEQS):
                for c in range(CC):
                    last = v.tensor_tensor(acc[:, c, t0:t0 + length], acc[:, c, t0:t0 + length], mean[s][:, 0:length],
                                           ALU.subtract)
                last.then_inc(free(("mean", s)), 1)
            for i in ROT_DVE[2:]:
                rotate(dve, v, i, rtmp_d, link)
            for s in range(2):
                was_read(dve, ("var", s))
            link(v.reciprocal(cstd, cstd))
            for c in range(CC):
                v.tensor_tensor(acc[:, c, :], acc[:, c, :], cstd, ALU.mult).then_inc(conv_norm, 1)

            def softmax(kind, units, u0):
                wide = 4 if kind == "s" else 2

                def inverse(u):
                    was_read(dve, (kind + "S", u))
                    v.reciprocal(rinv[:, u % 4:u % 4 + 1], rsum[:, u % 4:u % 4 + 1]).then_inc(inv_ready, 1)

                def turned(u):
                    n, s, h, i, width = units[u]
                    key = (kind + "T", u)
                    bank = full(dve, key)
                    if n >= 2:
                        full(dve, (kind + "O", n - 2, 0 if kind == "s" else 1))
                    m = width // P
                    v.tensor_copy(PT[n % 2][:, 0:m, i * P:(i + 1) * P],
                                  bank[:, 0:width].rearrange("p (k t) -> p k t", k=m)).then_inc(free(key), 1)

                for u, (n, s, h, i, width) in enumerate(units):
                    bank = full(dve, (kind + "S", u))
                    if u >= 4:
                        was_read(dve, (kind + "S", u - 4))
                    v.tensor_reduce(nmax[:, u % 4:u % 4 + 1], bank[:, 0:width], AX.X, ALU.max,
                                    negate=True).then_inc(max_ready, 1)
                    if u >= 1:
                        inverse(u - 1)
                    if u >= S_AHEAD:
                        turned(u - S_AHEAD)
                inverse(len(units) - 1)
                for u in range(len(units) - S_AHEAD, len(units)):
                    turned(u)

            softmax("s", SELF, 0)

            def residual(key, i, j):
                bank = full(dve, key)
                rows = hres[:, i, 512 * j:512 * (j + 1)]
                return v.scalar_tensor_tensor(out=rows, in0=rows, scalar=ALPHA, in1=bank, op0=ALU.mult, op1=ALU.add)

            order = sorted(LN_1 + LN_M)
            for k, n in enumerate(order):
                if n in LN_1:
                    i = LN_1.index(n)
                    for j in range(2):
                        residual(("mix", i, j), i, j).then_inc(free(("mix", i, j)), 1)
                        was_read(dve, ("mix", i, j))
                else:
                    i = LN_M.index(n)
                    dve.wait_ge(mem_in[i % 2], 16 * (i // 2 + 1))
                dve_stats(dve, n, link)
                if k >= 2:
                    dve_bias(dve, order[k - 2], link)
            for n in order[-2:]:
                dve_bias(dve, n, link)
            softmax("x", CROSS, len(SELF))
            for k, n in enumerate(LN_2):
                if k >= 1:
                    dve_bias(dve, LN_2[k - 1], link)
                for j in range(2):
                    residual(("co", k, j), k, j).then_inc(free(("co", k, j)), 1)
                    was_read(dve, ("co", k, j))
                dve_stats(dve, n, link)
            dve_bias(dve, LN_2[-1], link)

            dve.wait_ge(small_in, 32)
            bank = full(dve, "route")
            v.tensor_tensor(lg, bank[:, 0:NT * NR].rearrange("p (t n) -> p t n", t=NT),
                            br.rearrange("p (a n) -> p a n", a=1).to_broadcast([P, NT, NR]),
                            ALU.add).then_inc(free("route"), 1)
            was_read(dve, "route")
            dve.wait_ge(route_const, 9)

            def over(a, n):
                return a.rearrange("p (t a) -> p t a", a=1).to_broadcast([P, NT, n])

            def along(a, n):
                return a.rearrange("p (a e) -> p a e", a=1).to_broadcast([P, NT, n])

            def first_max(vals, n, top, mask, tmp, out):
                link(v.tensor_reduce(top, vals, AX.X, ALU.max))
                link(v.tensor_tensor(mask, vals, over(top, n), ALU.is_equal))
                link(v.tensor_tensor(mask, mask, along(desc[:, EPG - n:EPG], n), ALU.mult))
                link(v.tensor_reduce(tmp, mask, AX.X, ALU.max))
                link(v.tensor_tensor(out, mask, over(tmp, n), ALU.is_equal))

            gl, el = lg[:, :, 0:GROUPS], lg[:, :, GROUPS:NR]
            first_max(gl, GROUPS, gmx, geq, gm2, G)
            v.tensor_tensor(gex, gl, over(gmx, GROUPS), ALU.subtract).then_inc(route_dve, 1)
            gw = G.rearrange("p t (g a) -> p t g a", a=1).to_broadcast([P, NT, GROUPS, EPG])
            link(v.tensor_tensor(esel4, el.rearrange("p t (g e) -> p t g e", g=GROUPS), gw, ALU.mult))
            link(v.tensor_reduce(esel, esel4.rearrange("p t g e -> p t e g"), AX.X, ALU.add))
            first_max(esel, EPG, v1, eq, m1, H1)
            link(v.scalar_tensor_tensor(out=e2, in0=H1, scalar=-3.0e38, in1=esel, op0=ALU.mult, op1=ALU.add))
            first_max(e2, EPG, v2, eq, m2, H2)
            v.tensor_tensor(ev, v2, v1, ALU.subtract).then_inc(route_dve, 1)
            v.tensor_tensor(e2, H1, H2, ALU.add).then_inc(route_dve, 1)
            dve.wait_ge(route_dve, 3)

            def at_expert(out, H):
                return v.tensor_tensor(out, H.rearrange("p t (a e) -> p t a e", a=1).to_broadcast([P, NT, GROUPS, EPG]),
                                       gw, ALU.mult)

            at_expert(both.rearrange("p t (g e) -> p t g e", g=GROUPS), e2).then_inc(route_dve, 1)
            dve.wait_ge(route_dve, 4)
            for i in range(NT):
                last = v.tensor_reduce(upto[:, i, :], both[:, 0:i + 1, :].rearrange("p t e -> p e t"), AX.X, ALU.add)
            last.then_inc(route_dve, 1)
            at_expert(pick[0], H1)
            link(at_expert(pick[1], H2))
            pk = [q.rearrange("p t g e -> p t (g e)") for q in pick]
            for k in range(2):
                for n, rows in enumerate((tokf, (tokf, pairf)[k])):
                    v.tensor_tensor(held[k][:, :, n, :], pk[k], over(rows, NE), ALU.mult)
            bank = full(dve, "rank")
            ranks = bank[:, 0:NT * NE].rearrange("p (t e) -> p t e", t=NT)
            for k in range(2):
                link(v.tensor_tensor(rkp, ranks, pk[k], ALU.mult))
                link(v.tensor_reduce(rankf[k], rkp, AX.X, ALU.add))
                v.tensor_tensor(hot[k], along(riota, P), over(rankf[k], P), ALU.is_equal).then_inc(hot_ready, 1)
            first = full(dve, "first")
            v.tensor_scalar(tab0[:, :], first[:, 0:2 * NE], float(BIG), None, ALU.add).then_inc(tab0_ready, 1)
            link(v.scalar_tensor_tensor(out=rk, in0=ranks,
                                        scalar=float(NE), in1=along(eiota, NE), op0=ALU.mult, op1=ALU.add))
            for k in range(2):
                link(v.tensor_tensor(rkp, rk, pk[k], ALU.mult))
                link(v.tensor_reduce(slotf, rkp, AX.X, ALU.add))
                v.tensor_copy(slots[:, k, :], slotf).then_inc(slots_ready, 1)
                dve.wait_ge(slots_ready, k + 1)
            dve.wait_ge(route_exp, 2)
            link(v.tensor_reduce(gsum, gex, AX.X, ALU.add))
            link(v.reciprocal(pgrp, gsum))
            link(v.tensor_scalar(den, ev, 1.0, None, ALU.add))
            link(v.reciprocal(den, den))
            link(v.tensor_tensor(pw[:, 0, :], pgrp, den, ALU.mult))
            link(v.tensor_tensor(pw[:, 1, :], pw[:, 0, :], ev, ALU.mult))
            bank = full(dve, "count")
            link(v.tensor_copy(cnt[0:NE], bank[0:NE, 0:1]))
            link(v.tensor_scalar(more[0:NE], thr[0:NE], cnt[0:NE], None, ALU.is_lt))
            v.tensor_reduce(cnt[0:NE], more[0:NE], AX.X, ALU.add).then_inc(counts_in, 1)
            bank = full(dve, "base")
            link(v.tensor_copy(base[0:NE], bank[0:NE, 0:1]))
            link(v.tensor_scalar(hitm[0:NE], jb[0:NE], base[0:NE], None, ALU.is_equal))
            v.tensor_tensor(hitm[0:NE], hitm[0:NE],
                            more[0:NE].rearrange("p (b a) -> p b a", a=1).to_broadcast([NE, BLOCKS - 1, LIST]),
                            ALU.mult).then_inc(counts_in, 1)
            bank = full(dve, "list")
            w = (BLOCKS - 1) * LIST
            link(v.tensor_copy(lst[0:1], bank[0:1, 0:2 * w]))
            le = lst[0:1, 0:w].rearrange("p (b j) -> p j b", j=LIST)
            l1 = lst[0:1, w:2 * w].rearrange("p (b j) -> p b j", j=LIST)
            link(v.tensor_tensor(lstb[0:1].rearrange("p (b j) -> p b j", j=LIST), l1,
                                 bcol[0:1].rearrange("p (b a) -> p b a", a=1).to_broadcast([1, BLOCKS - 1, LIST]),
                                 ALU.mult))
            link(v.tensor_reduce(res[0:1, 0:1], lst[0:1, w:2 * w], AX.X, ALU.add))
            link(v.tensor_reduce(res[0:1, 1:1 + LIST], le, AX.X, ALU.add))
            link(v.tensor_reduce(res[0:1, 1 + LIST:1 + 2 * LIST], lstb[0:1].rearrange("p (b j) -> p j b", j=LIST),
                                 AX.X, ALU.add))
            link(v.scalar_tensor_tensor(out=res[0:1, 1 + LIST:1 + 2 * LIST], in0=res[0:1, 1 + LIST:1 + 2 * LIST],
                                        scalar=float(BLOCKS * NE), in1=res[0:1, 1:1 + LIST], op0=ALU.add, op1=ALU.add))
            v.tensor_copy(ctl[:, :], res[0:1, :]).then_inc(ctl_ready, 1)

            def block_dve_T(j, b):
                dve.wait_ge(rowsT_full, j + 1)
                v.tensor_copy(xT[b][:, 4:8, :], ps[:, 5, :].rearrange("p (k t) -> p k t", k=4)).then_inc(rowsT_d, 1)

            def block_dve(j, b, uses):
                if later(uses):
                    dve.wait_ge(down_full, j - 1)
                dve.wait_ge(silu_done, j + 1)
                v.tensor_tensor(hid[b], act_g[b], ps[:, b, 256:512].rearrange("p (k t) -> p k t", k=2),
                                ALU.mult).then_inc(hid_ready, 1)

            def block_dve_out(j, b, uses):
                dve.wait_ge(down_full, j + 1)
                if later(uses):
                    dve.wait_ge(rows_out[b], 16 * uses)
                v.tensor_copy(yo[b][:, 512:1024], ps[:, 3 + 4 * b, :]).then_inc(yo_d, 1)

            def blocks(j0, n, half, end=False):
                for b in range(n):
                    block_dve(j0 + b, b % 2, half + b // 2)
                    if not (end and b == n - 1):
                        block_dve_T(j0 + b + 1, (b + 1) % 2)
                    block_dve_out(j0 + b, b % 2, half + b // 2)

            block_dve_T(0, 0)
            blocks(0, NB, 0)
            with dve.Fori(1, NE // NB - 1) as i:
                blocks(NB * i, NB, 2 * i)
            blocks(NE - NB, NB + STEADY - NE, (NE - NB) // 2, end=True)
            dve.wait_ge(ctl_ready, 1)
            n_over = dve.value_load(ctl[0:1, 0:1], min_val=0, max_val=LIST)
            with dve.Fori(1, PAIRS_OVER) as i:
                with dve.If(2 * i < n_over):
                    for b in range(2):
                        block_dve_T(NE + 2 * i + b, b)
                        block_dve(NE + 2 * i + b, b, NE // 2 + i)
                        block_dve_out(NE + 2 * i + b, b, NE // 2 + i)

            def add_choice(k, c):
                dve.wait_ge(prow_in[2 * k + c], 16)
                if c == 1:
                    dve.wait_ge(summed, 2 * k + 1)
                v.scalar_tensor_tensor(out=hres[:, k, :], in0=prow[2 * k + c], scalar=pw[:, c, k:k + 1],
                                       in1=hres[:, k, :], op0=ALU.mult, op1=ALU.add).then_inc(summed, 1)

            dve.wait_ge(scaled, NT)
            add_choice(0, 0)
            for k, n in enumerate(LN_3):
                add_choice(k, 1)
                if k + 1 < NT:
                    add_choice(k + 1, 0)
                dve.wait_ge(summed, 2 * k + 2)
                dve_stats(dve, n, link)
                if k >= 2:
                    dve_bias(dve, LN_3[k - 2], link)
            for n in LN_3[-2:]:
                dve_bias(dve, n, link)

        @block.tensor
        def _(pe):
            t = nc.tensor

            def claim(key):
                b, n = place[key]
                if n:
                    pe.wait_ge(bank_free[b], n)
                return ps[:, b, :]

            def done(key, last):
                last.then_inc(bank_full[place[key][0]], 1)

            def slab(name):
                n = slab_names.index(name)
                pe.wait_ge(slab_in[n % 3], 16 * (n // 3 + 1))
                w = w_slabs[n][1].shape[1]
                return ring[:, n % 3, 0:KC * w].rearrange("p (k c) -> p k c", k=KC)

            def product(key, out_of, lhs, rhs):
                bank = claim(key)
                for k in range(KC):
                    last = t.matmul(out_of(bank), lhs(k), rhs(k), start=(k == 0), stop=(k == KC - 1))
                return last

            def rows_T(layer, i, rows, n):
                pe.wait_ge(ln_done, n + 1)
                for j in range(2):
                    key = ("mT", i, j) if layer == "m" else ("hT", layer, i, j)
                    bank = claim(key)
                    for c in range(4):
                        last = t.transpose(bank[:, c * P:(c + 1) * P], rows[:, (4 * j + c) * P:(4 * j + c + 1) * P],
                                           ident[:, :])
                    done(key, last)

            def gates(c, s):
                t0, length = SEQS[s]
                for name, w in (("a", wa), ("g", wg)):
                    last = product((name, c, s), lambda k: k[:, 0:length], lambda k: w[:, k, c * P:(c + 1) * P],
                                   lambda k: hTv[:, k, t0:t0 + length])
                    done((name, c, s), last)

            pe.wait_ge(const_ready, 1)
            for i in range(2):
                rows_T(0, i, hres[:, i, :], LN_X[i])
            for j in range(2):
                was_read(pe, ("hT", 0, 1, j))
            wa, wg = (ring[:, n, :].rearrange("p (k c) -> p k c", k=KC) for n in range(2))
            pe.wait_ge(first_in, 32)
            gates(0, 0)
            for i in range(2, NT):
                rows_T(0, i, hres[:, i, :], LN_X[i])
            pe.wait_ge(conv_in, 16)
            bank = claim("cpar")
            for c in range(CC):
                last = t.transpose(bank[:, c * (TAPS + 3):(c + 1) * (TAPS + 3)], cpar_in[:, c * P:(c + 1) * P],
                                   ident[0:TAPS + 3, 0:TAPS + 3])
            done("cpar", last)
            for j in range(2):
                was_read(pe, ("hT", 0, NT - 1, j))
            gates(0, 1)
            wa, wg = slab("a"), slab("g")
            for c in range(1, CC):
                for s in range(2):
                    gates(c, s)

            def qk_T(i):
                rotated(pe, i)
                bank = claim(("qT", i))
                for c in range(PAIRS):
                    last = t.transpose(bank[:, c * P:(c + 1) * P], rot[i % 4][:, c * P:(c + 1) * P], ident[:, :])
                done(("qT", i), last)
                bank = claim(("kT", i))
                last = t.transpose(bank[:, 0:P], rot[i % 4][:, PAIRS * P:(PAIRS + 1) * P], ident[:, :])
                done(("kT", i), last)

            wq, wkv = slab("q"), slab("kv")
            for i in range(NT):
                for name, w, n in (("q", wq, 512), ("kv", wkv, 256)):
                    last = product((name, i), lambda k: k[:, 0:n], lambda k: hTv[:, k, i * P:(i + 1) * P],
                                   lambda k: w[:, k, :])
                    done((name, i), last)
                for m in QKT_AFTER.get(i, ()):
                    qk_T(m)
                for what in ("mean", "var"):
                    if i == CONV_AFTER[what]:
                        for s, (t0, length) in enumerate(SEQS):
                            if what == "mean":
                                pe.wait_ge(conv_done[s], CC * (TAPS - 1 + s))
                            else:
                                pe.wait_ge(conv_sq, s + 1)
                            bank = claim((what, s))
                            for c in range(CC):
                                last = t.matmul(bank[:, 0:length], ones_c[:, :],
                                                (acc if what == "mean" else convsq)[:, c, t0:t0 + length],
                                                start=(c == 0), stop=(c == CC - 1))
                            done((what, s), last)
            for m in (NT - 2, NT - 1):
                qk_T(m)

            def attention(kind, units, u0, n0):
                def scores(u):
                    n, s, h, i, width = units[u]
                    bank = claim((kind + "S", u))
                    t0 = SEQS[s][0] + i * P
                    if kind == "s":
                        half = h // PAIRS * HD
                        last = t.matmul(bank[:, 0:width], qT[half:half + HD, h % PAIRS, t0:t0 + P],
                                        kT[half:half + HD, SEQS[s][0]:SEQS[s][0] + width], start=True, stop=True)
                    else:
                        for j in range(2):
                            last = t.matmul(bank[:, 0:width], catv[:, 2 * h + j, t0:t0 + P],
                                            kmT[:, 2 * h + j, s * N_MEM:(s + 1) * N_MEM], start=(j == 0), stop=(j == 1))
                    done((kind + "S", u), last)

                def turn(u):
                    width = units[u][4]
                    bank = claim((kind + "T", u))
                    pe.wait_ge(prob_ready, u0 + u + 1)
                    for k in range(width // P):
                        last = t.transpose(bank[:, k * P:(k + 1) * P], prob[u % 4][:, k * P:(k + 1) * P], ident[:, :])
                    done((kind + "T", u), last)

                def values(n):
                    us = [u for u in range(len(units)) if units[u][0] == n]
                    _, s, h, _, width = units[us[0]]
                    length = SEQS[s][1]
                    for u in us[-2:]:
                        was_read(pe, (kind + "T", u))
                    for j in range(1 if kind == "s" else 2):
                        key = (kind + "O", n, j)
                        claim(key)
                        b = place[key][0]
                        for k in range(width // P):
                            if kind == "s":
                                half = h % 2 * HD
                                out = ps[half:half + HD, b, 0:length]
                                lhs = vtok[:, SEQS[s][0] // P + k, h // PAIRS * HD:(h // PAIRS + 1) * HD]
                            else:
                                out = ps[:, b, 0:length]
                                lhs = vm[:, s * N_MEM // P + k, h * MHD + j * P:h * MHD + (j + 1) * P]
                            last = t.matmul(out, lhs, PT[n % 2][:, k, 0:length], start=(k == 0),
                                            stop=(k == width // P - 1))
                        done(key, last)

                pending = []
                for u in range(len(units) + S_AHEAD):
                    if u < len(units):
                        scores(u)
                    if u >= S_AHEAD:
                        turn(u - S_AHEAD)
                    for n in pending:
                        values(n)
                    pending = []
                    k = u - S_AHEAD
                    if k >= 0 and (k + 1 == len(units) or units[k + 1][0] != units[k][0]):
                        pending.append(units[k][0])
                for n in pending:
                    values(n)

            was_read(pe, ("qT", NT - 1))
            was_read(pe, ("kT", NT - 1))
            was_read(pe, ("kv", NT - 1))
            attention("s", SELF, 0, 0)

            wm = [slab("mix0"), slab("mix1")]
            pe.wait_ge(conv_out, CC)
            for n in range(SELF[-1][0] + 1)[-2:]:
                was_read(pe, ("sO", n, 0))
            for i in range(NT):
                for j in range(2):
                    last = product(("mix", i, j), lambda k: k, lambda k: catv[:, k, i * P:(i + 1) * P],
                                   lambda k: wm[j][:, k, :])
                    done(("mix", i, j), last)
                    if i >= 2 and j == 0:
                        rows_T(1, i - 2, hres[:, i - 2, :], LN_1[i - 2])
                    elif i >= 2:
                        rows_T("m", i - 2, mrow[i % 2], LN_M[i - 2])

            for j in range(2):
                was_read(pe, ("mT", MT - 1, j))
            for c in range(KC):
                w = slab(f"ck{c // 4}")
                last = product(("ck", c), lambda k: k, lambda k: w[:, k, c % 4 * P:(c % 4 + 1) * P], lambda k: mT[:, k, :])
                done(("ck", c), last)
            wv = [slab("cv0"), slab("cv1")]
            for i in range(MT):
                for j in range(2):
                    last = product(("cv", i, j), lambda k: k, lambda k: mT[:, k, i * P:(i + 1) * P],
                                   lambda k: wv[j][:, k, :])
                    done(("cv", i, j), last)
            for i in range(MT, NT):
                rows_T(1, i, hres[:, i, :], LN_1[i])
            for j in range(2):
                was_read(pe, ("hT", 1, NT - 1, j))
            for c in range(KC):
                w = slab(f"cq{c // 4}")
                for s, (t0, length) in enumerate(SEQS):
                    last = product(("cq", c, s), lambda k: k[:, 0:length], lambda k: w[:, k, c % 4 * P:(c % 4 + 1) * P],
                                   lambda k: hTv[:, k, t0:t0 + length])
                    done(("cq", c, s), last)
            for s in range(2):
                was_read(pe, ("cq", KC - 1, s))
            attention("x", CROSS, len(SELF), SELF[-1][0] + 1)
            wo = [slab("co0"), slab("co1")]
            for j in range(2):
                was_read(pe, ("xO", CROSS[-1][0], j))

            def route(i):
                for j in range(2):
                    was_read(pe, ("hT", 2, i, j))
                for k in range(KC):
                    last = t.matmul(logits[:, i * NR:(i + 1) * NR], catv[:, k, i * P:(i + 1) * P], wr[:, k, :],
                                    start=(k == 0), stop=(k == KC - 1))
                return last

            pe.wait_ge(small_in, 32)
            logits = claim("route")
            for i in range(NT + 1):
                if i < NT:
                    for j in range(2):
                        last = product(("co", i, j), lambda k: k, lambda k: hTv[:, k, i * P:(i + 1) * P],
                                       lambda k: wo[j][:, k, :])
                        done(("co", i, j), last)
                if i >= 1:
                    rows_T(2, i - 1, hres[:, i - 1, :], LN_2[i - 1])
                if 2 <= i < NT:
                    route(i - 2)
                if i == NT - 1:
                    route(i - 1)
            done("route", route(NT - 1))

            pe.wait_ge(route_dve, 5)
            bank = claim("rank")
            t.matmul(bank[:, 0:NT * NE], before[:, :], both.rearrange("p t e -> p (t e)"), start=True, stop=False)
            last = t.matmul(bank[:, NE:NT * NE], ones[:, :], upto[:, 0:NT - 1, :].rearrange("p t e -> p (t e)"),
                            start=False, stop=True)
            done("rank", last)
            bank = claim("first")
            for k in range(2):
                pe.wait_ge(hot_ready, k + 1)
                for i in range(NT):
                    last = t.matmul(bank[:, 0:2 * NE], hot[k][:, i, :], held[k][:, i, :, :].rearrange("p a e -> p (a e)"),
                                    start=(k == 0 and i == 0), stop=(k == 1 and i == NT - 1))
            done("first", last)
            bank = claim("count")
            last = t.matmul(bank[0:NE, 0:1], upto[:, NT - 1, :], ones[:, 0:1], start=True, stop=True)
            done("count", last)
            pe.wait_ge(counts_in, 1)
            bank = claim("base")
            last = t.matmul(bank[0:NE, 0:1], before[0:NE, 0:NE], cnt[0:NE], start=True, stop=True)
            done("base", last)
            pe.wait_ge(counts_in, 2)
            bank = claim("list")
            w = (BLOCKS - 1) * LIST
            hits = hitm[0:NE].rearrange("p b j -> p (b j)")
            t.matmul(bank[0:1, 0:w], ecol[0:NE, 0:1], hits, start=True, stop=True)
            last = t.matmul(bank[0:1, w:2 * w], ones[0:NE, 0:1], hits, start=True, stop=True)
            done("list", last)

            def block_T(j, b, r, uses):
                pe.wait_ge(rows_in[r], 16 * (uses + 1))
                if later(j):
                    pe.wait_ge(rowsT_a, j)
                    pe.wait_ge(rowsT_d, j)
                for c in range(KC):
                    last = t.transpose(ps[:, 4 + c // 4, c % 4 * P:(c % 4 + 1) * P], xg[r][:, c:D:KC],
                                       ident[:, :])
                last.then_inc(rowsT_full, 1)

            def block_gu(j, b, r, uses, half):
                pe.wait_ge(rowsT_a, j + 1)
                pe.wait_ge(rowsT_d, j + 1)
                pe.wait_ge(wexp_in[r], 48 * (uses + 1))
                if later(half):
                    pe.wait_ge(hid_ready, j - 1)
                for m, off in ((0, 0), (1, 2048)):
                    w = wexp[r][:, off:off + 2048].rearrange("p (k f) -> p k f", k=KC)
                    for f in range(2):
                        for k in range(KC):
                            last = t.matmul(ps[:, b, (2 * m + f) * P:(2 * m + f + 1) * P], w[:, k, f:FE:2],
                                            xT[b][:, k, :], start=(k == 0), stop=(k == KC - 1))
                last.then_inc(gu_full, 1)

            def block_down(j, b, r, half):
                pe.wait_ge(hid_ready, j + 1)
                if later(half):
                    pe.wait_ge(yo_a, j - 1)
                    pe.wait_ge(yo_d, j - 1)
                w = wexp[r][:, 4096:6144].rearrange("p (k f) -> p k f", k=2)
                for n in range(2):
                    for k in range(2):
                        last = t.matmul(ps[:, 2 + n + 4 * b, :], hid[b][:, k, :], w[:, k, n * 512:(n + 1) * 512],
                                        start=(k == 0), stop=(k == 1))
                last.then_inc(down_full, 1)

            def blocks(j0, n, q, half, end=False):
                for b in range(n):
                    block_gu(j0 + b, b % 2, b % NB, q + b // NB, half + b // 2)
                    if not (end and b == n - 1):
                        block_T(j0 + b + 1, (b + 1) % 2, (b + 1) % NB, q + (b + 1) // NB)
                    block_down(j0 + b, b % 2, b % NB, half + b // 2)

            block_T(0, 0, 0, 0)
            blocks(0, NB, 0, 0)
            with pe.Fori(1, NE // NB - 1) as i:
                blocks(NB * i, NB, i, 2 * i)
            blocks(NE - NB, NB + STEADY - NE, NE // NB - 1, (NE - NB) // 2, end=True)
            pe.wait_ge(ctl_ready, 1)
            n_over = pe.value_load(ctl[0:1, 0:1], min_val=0, max_val=LIST)
            with pe.Fori(1, PAIRS_OVER) as i:
                with pe.If(2 * i < n_over):
                    for b in range(2):
                        block_T(NE + 2 * i + b, b, b, NE // NB + i)
                        block_gu(NE + 2 * i + b, b, b, NE // NB + i, NE // 2 + i)
                        block_down(NE + 2 * i + b, b, b, NE // 2 + i)


def rope_tables():
    import numpy as np

    n = max(length for _, length in SEQS)
    t = np.arange(n)
    freq = (np.float32(10000.0) ** (-np.arange(0, 32, 2, dtype=np.float32) / np.float32(32))).astype(np.float32)
    ang = np.concatenate([(t // 64).astype(np.float32)[:, None] * freq,
                          (t % 64).astype(np.float32)[:, None] * freq], -1)
    return np.cos(ang).astype(np.float32), np.sin(ang).astype(np.float32)


def kernel(**inputs):
    import numpy as np
    import concourse.bacc as bacc
    from concourse.bass_utils import run_bass_kernel_spmd

    a = {k: np.asarray(v) for k, v in inputs.items()}
    cos, sin = rope_tables()
    arrays = {
        "x": np.concatenate([a["x_prompt"][0], a["x_sample"][0]]),
        "mem": np.concatenate([a["mem_prompt"][0], a["mem_sample"][0]]),
        "lnp": np.stack([a["ln_in_g"], a["ln_in_b"], a["ln1_g"][0], a["ln1_b"][0], a["ln2_g"][0], a["ln2_b"][0],
                         a["ln3_g"][0], a["ln3_b"][0], a["ln_mem_g"], a["ln_mem_b"]]),
        "rope_cos": cos, "rope_sin": sin, "q_gain": a["q_norm_g"][0], "k_gain": a["k_norm_g"][0],
        "conv_rows": np.concatenate([a["conv_w"][0], a["conv_b"], a["conv_ln_g"], a["conv_ln_b"]]),
        "w_router": np.concatenate([a["w_router_g"][0], a["w_router_e"][0].transpose(1, 0, 2).reshape(D, NE)], 1)
        .reshape(KC, P, NR).transpose(1, 0, 2),
        "b_router": np.concatenate([a["b_router_g"][0], a["b_router_e"][0].reshape(NE)]),
        "w_gate": a["w_e_gate"][0], "w_up": a["w_e_up"][0], "w_down": a["w_e_down"][0],
    }
    for name in ("w_in", "w_mix_out", "w_cq", "w_ck", "w_cv", "w_co"):
        arrays[name] = a[name][0]
    arrays = {k: np.ascontiguousarray(v) for k, v in arrays.items()}
    nc = bacc.Bacc("TRN2", target_bir_lowering=False, num_devices=1)
    d = {k: nc.dram_tensor(k, v.shape, mybir.dt.from_np(v.dtype), kind="ExternalInput").ap() for k, v in arrays.items()}
    y = nc.dram_tensor("y", (T, D), F32, kind="ExternalOutput").ap()
    slabs = weight_slabs(d["w_in"], d["w_mix_out"], d["w_ck"], d["w_cv"], d["w_cq"], d["w_co"])
    lnp = [d["lnp"][n] for n in range(10)]
    encoder(nc, d["x"], d["mem"], slabs, lnp, d["rope_cos"], d["rope_sin"], d["q_gain"], d["k_gain"], d["conv_rows"],
            d["w_router"], d["b_router"], d["w_gate"], d["w_up"], d["w_down"], y)
    r = run_bass_kernel_spmd(nc, [arrays], core_ids=[0])
    out = r.results[0]["y"]
    return out[0:256].reshape(1, 256, D), out[256:768].reshape(1, 512, D)
```
